# Optimizing a Trainium2 kernel written in Bass

```python
import math
import jax, jax.numpy as jnp
from jax import lax
import numpy as np

D_MODEL = 1024
BATCH = 1
SEQ = 256
DEPTH = 1

HEAD_DIM = 64
POOL_WIDTH = D_MODEL // 4
POOL_WINDOWS = (2, 4, 8, 16)
POOL_GROUPS = len(POOL_WINDOWS)
POOL_GROUP_DIM = POOL_WIDTH // POOL_GROUPS
ATTN_WIDTH = D_MODEL - POOL_WIDTH
ATTN_HEADS = ATTN_WIDTH // HEAD_DIM
DILATION_CFG = ((128, 1), (512, 4), (2048, 16))
N_DIL = len(DILATION_CFG)
HEADS_PER_DIL = ATTN_HEADS // N_DIL
ATTN_OUT_WIDTH = HEADS_PER_DIL * HEAD_DIM
IN_PROJ_WIDTH = POOL_WIDTH + 3 * ATTN_WIDTH
OUT_PROJ_WIDTH = POOL_WIDTH + ATTN_OUT_WIDTH
ROT_DIM = HEAD_DIM // 4
ROPE_THETA = 500000.0
D_FF = 11 * D_MODEL // 4
CONV_WIDTH = 3
BLOCK = 128
NORM_EPS = 1e-6
N_MOD = 6


def rms_norm(x, g):
    x32 = x.astype(jnp.float32)
    y = x32 * lax.rsqrt(jnp.mean(x32 * x32, axis=-1, keepdims=True) + NORM_EPS)
    return (y * g.astype(jnp.float32)).astype(x.dtype)

def partial_rope(t, cos, sin):
    half = ROT_DIM // 2
    t1 = t[..., :half]
    t2 = t[..., half:ROT_DIM]
    return jnp.concatenate(
        [t1 * cos - t2 * sin, t2 * cos + t1 * sin, t[..., ROT_DIM:]], axis=-1)

def causal_multiscale_pool(u, w_pool, b_pool, pool_scale):
    B, S, _ = u.shape
    u32 = u.astype(jnp.float32).reshape(B, S, POOL_GROUPS, POOL_GROUP_DIM)
    cs = jnp.cumsum(u32, axis=1)
    t = jnp.arange(S, dtype=jnp.float32)
    means = []
    for gi, w in enumerate(POOL_WINDOWS):
        csg = cs[:, :, gi]
        lagged = jnp.pad(csg[:, :S - w], ((0, 0), (w, 0), (0, 0)))
        count = jnp.minimum(t + 1.0, float(w))
        means.append((csg - lagged) / count[None, :, None])
    mixed = jnp.stack(means, axis=2) - u32
    y = jnp.einsum('bsgc,gcd->bsgd', mixed, w_pool.astype(jnp.float32)) + b_pool.astype(jnp.float32)
    return (y.reshape(B, S, POOL_WIDTH) * pool_scale.astype(jnp.float32)).astype(u.dtype)

def dilated_window_attention(q, k, v, window, dilation):
    B, S, H, hd = q.shape
    span = window // dilation
    assert span <= BLOCK
    chunk = dilation * BLOCK
    s_pad = -(-S // chunk) * chunk
    padw = ((0, 0), (0, s_pad - S), (0, 0), (0, 0))
    q, k, v = (jnp.pad(a.astype(jnp.float32), padw) for a in (q, k, v))
    nb = s_pad // chunk
    qb, kb, vb = (a.reshape(B, nb, BLOCK, dilation, H, hd) for a in (q, k, v))

    def with_prev(a):
        prev = jnp.pad(a[:, :-1], ((0, 0), (1, 0), (0, 0), (0, 0), (0, 0), (0, 0)))
        return jnp.concatenate([prev, a], axis=2)

    kk, vv = with_prev(kb), with_prev(vb)
    scores = jnp.einsum('bnirhd,bnjrhd->bnrhij', qb, kk)
    i = jnp.arange(BLOCK)[:, None]
    j = jnp.arange(2 * BLOCK)[None, :]
    n = jnp.arange(nb)[:, None, None]
    dist = BLOCK + i - j
    valid = (dist >= 0) & (dist <= span) & (n * BLOCK + j - BLOCK >= 0)
    scores = jnp.where(valid[None, :, None, None], scores, -jnp.inf)
    m = jnp.max(scores, axis=-1, keepdims=True)
    p = jnp.exp(scores - m)
    den = jnp.sum(p, axis=-1)
    o = jnp.einsum('bnrhij,bnjrhd->bnirhd', p, vv)
    den_t = jnp.moveaxis(den, -1, 2)
    lse_t = jnp.moveaxis(m[..., 0] + jnp.log(den), -1, 2)
    o = (o / den_t[..., None]).reshape(B, s_pad, H, hd)[:, :S]
    lse = lse_t.reshape(B, s_pad, H)[:, :S]
    return o, lse

def mixing_sublayer(h, cos, sin, w_in, w_pool, b_pool, pool_scale, w_out):
    B, S, _ = h.shape
    proj = h @ w_in
    u_pool = proj[..., :POOL_WIDTH]
    qkv = proj[..., POOL_WIDTH:].reshape(B, S, 3, ATTN_HEADS, HEAD_DIM)
    q = partial_rope(qkv[:, :, 0], cos, sin) * (HEAD_DIM ** -0.5)
    k = partial_rope(qkv[:, :, 1], cos, sin)
    v = qkv[:, :, 2]
    outs, lses = [], []
    for g, (window, dilation) in enumerate(DILATION_CFG):
        sl = slice(g * HEADS_PER_DIL, (g + 1) * HEADS_PER_DIL)
        o, l = dilated_window_attention(q[:, :, sl], k[:, :, sl], v[:, :, sl], window, dilation)
        outs.append(o)
        lses.append(l)
    alpha = jax.nn.softmax(jnp.stack(lses, axis=0), axis=0)
    attn = jnp.sum(alpha[..., None] * jnp.stack(outs, axis=0), axis=0)
    attn = attn.reshape(B, S, ATTN_OUT_WIDTH).astype(h.dtype)
    pool = causal_multiscale_pool(u_pool, w_pool, b_pool, pool_scale)
    return jnp.concatenate([pool, attn], axis=-1) @ w_out

def conv_ffn(h, w_up, conv_w, conv_b, w_down):
    S = h.shape[1]
    up = h @ w_up
    gate, val = up[..., :D_FF], up[..., D_FF:]
    gp = jnp.pad(gate, ((0, 0), (CONV_WIDTH - 1, 0), (0, 0)))
    gate = gp[:, 0:S] * conv_w[0] + gp[:, 1:S + 1] * conv_w[1] + gp[:, 2:S + 2] * conv_w[2] + conv_b
    return (jax.nn.gelu(gate, approximate=True) * val) @ w_down

def first_inputs(seed: int = 0) -> dict:
    key = jax.random.key(seed)
    ks = jax.random.split(key, 20)
    f32 = jnp.float32
    nrm = lambda k, shape, s: jax.random.normal(k, shape, f32) * s
    L = DEPTH
    return {
        "x": nrm(ks[0], (BATCH, SEQ, D_MODEL), 1.0),
        "c": nrm(ks[1], (BATCH, D_MODEL), 1.0),
        "positions": jnp.broadcast_to(jnp.arange(SEQ, dtype=jnp.int32), (BATCH, SEQ)),
        "w_ada": nrm(ks[2], (L, D_MODEL, N_MOD * D_MODEL), D_MODEL ** -0.5),
        "b_ada": nrm(ks[3], (L, N_MOD * D_MODEL), 0.02),
        "g_pre_mix": 1.0 + nrm(ks[4], (L, D_MODEL), 0.05),
        "g_post_mix": 1.0 + nrm(ks[5], (L, D_MODEL), 0.05),
        "g_pre_ffn": 1.0 + nrm(ks[6], (L, D_MODEL), 0.05),
        "g_post_ffn": 1.0 + nrm(ks[7], (L, D_MODEL), 0.05),
        "w_in": nrm(ks[8], (L, D_MODEL, IN_PROJ_WIDTH), D_MODEL ** -0.5),
        "w_pool": nrm(ks[9], (L, POOL_GROUPS, POOL_GROUP_DIM, POOL_GROUP_DIM), POOL_GROUP_DIM ** -0.5),
        "b_pool": nrm(ks[10], (L, POOL_GROUPS, POOL_GROUP_DIM), 0.02),
        "pool_scale": 1.0 + nrm(ks[11], (L, POOL_WIDTH), 0.05),
        "w_out": nrm(ks[12], (L, OUT_PROJ_WIDTH, D_MODEL), OUT_PROJ_WIDTH ** -0.5),
        "w_up": nrm(ks[13], (L, D_MODEL, 2 * D_FF), D_MODEL ** -0.5),
        "conv_w": nrm(ks[14], (L, CONV_WIDTH, D_FF), CONV_WIDTH ** -0.5),
        "conv_b": nrm(ks[15], (L, D_FF), 0.02),
        "w_down": nrm(ks[16], (L, D_FF, D_MODEL), D_FF ** -0.5),
    }

def first_block(x, c, positions, w_ada, b_ada, g_pre_mix, g_post_mix, g_pre_ffn, g_post_ffn,
              w_in, w_pool, b_pool, pool_scale, w_out, w_up, conv_w, conv_b, w_down):
    inv_freq = ROPE_THETA ** (-jnp.arange(0, ROT_DIM, 2, dtype=jnp.float32) / ROT_DIM)
    ang = positions.astype(jnp.float32)[..., None] * inv_freq
    cos = jnp.cos(ang)[:, :, None, :].astype(x.dtype)
    sin = jnp.sin(ang)[:, :, None, :].astype(x.dtype)
    c_act = jax.nn.silu(c)
    for l in range(DEPTH):
        mod = c_act @ w_ada[l] + b_ada[l]
        sh_m, sc_m, gt_m, sh_f, sc_f, gt_f = (t[:, None, :] for t in jnp.split(mod, N_MOD, axis=-1))
        h = rms_norm(x, g_pre_mix[l]) * (1.0 + sc_m) + sh_m
        y = mixing_sublayer(h, cos, sin, w_in[l], w_pool[l], b_pool[l], pool_scale[l], w_out[l])
        x = x + gt_m * rms_norm(y, g_post_mix[l])
        h = rms_norm(x, g_pre_ffn[l]) * (1.0 + sc_f) + sh_f
        y = conv_ffn(h, w_up[l], conv_w[l], conv_b[l], w_down[l])
        x = x + gt_f * rms_norm(y, g_post_ffn[l])
    return x


DEPTH_2 = 2

ROPE_THETA_2 = 10000.0
Q_BLOCK = 128

A_HEADS = 8
A_HEAD_DIM = 64
IDX_HEADS = 8
IDX_DIM = 64
DSA_TOPK_MAX = 256

B_HEADS = 8
B_HEAD_DIM = 64
MOBA_BLOCK = 256
MOBA_TOPK = 3
MOBA_Q_CHUNK = 16

EVEN_COLS = (A_HEADS * A_HEAD_DIM,
             A_HEAD_DIM,
             A_HEAD_DIM,
             IDX_HEADS * IDX_DIM,
             IDX_DIM,
             IDX_HEADS,
             B_HEADS * B_HEAD_DIM,
             B_HEADS * B_HEAD_DIM,
             B_HEADS * B_HEAD_DIM)
EVEN_IN_COLS = int(sum(EVEN_COLS))
EVEN_SPLITS = tuple(int(c) for c in np.cumsum(EVEN_COLS)[:-1])
EVEN_OUT_COLS = A_HEADS * A_HEAD_DIM + B_HEADS * B_HEAD_DIM

C_HEADS = 16
C_NOPE = 64
C_ROPE = 32
C_V = 64
C_Q_RANK = 768
C_KV_RANK = 256
C_IN_COLS = C_Q_RANK + C_KV_RANK + C_ROPE

PEER_HEADS = 8
PEER_NKEYS = 128
PEER_N_EXPERTS = PEER_NKEYS * PEER_NKEYS
PEER_QDIM = 256
PEER_TOPK_HALF = 16
PEER_TOPK = 16
PEER_CHUNK = 128

N_EVEN = (DEPTH_2 + 1) // 2
N_ODD = DEPTH_2 // 2


def rms_norm_2(x, g):
    xf = x.astype(jnp.float32)
    y = xf * lax.rsqrt(jnp.mean(xf * xf, axis=-1, keepdims=True) + NORM_EPS)
    return (y * g.astype(jnp.float32)).astype(x.dtype)

def rope_tables(positions, dim):
    inv = 1.0 / (ROPE_THETA_2 ** (jnp.arange(0, dim, 2, dtype=jnp.float32) / dim))
    ang = positions.astype(jnp.float32)[..., None] * inv
    return jnp.cos(ang)[:, :, None, :], jnp.sin(ang)[:, :, None, :]

def apply_rope(x, cos, sin):
    x1, x2 = jnp.split(x, 2, axis=-1)
    c = cos.astype(x.dtype)
    s = sin.astype(x.dtype)
    return jnp.concatenate([x1 * c - x2 * s, x1 * s + x2 * c], axis=-1)

def to_blocks(a, blk):
    b, s = a.shape[:2]
    return jnp.moveaxis(a.reshape((b, s // blk, blk) + a.shape[2:]), 1, 0)

def from_blocks(a):
    a = jnp.moveaxis(a, 0, 1)
    return a.reshape((a.shape[0], a.shape[1] * a.shape[2]) + a.shape[3:])

def dsa_attention(q, k, v, iq, ik, iw):
    b, s = q.shape[:2]
    n_sel = min(DSA_TOPK_MAX, s // 4)
    key_pos = jnp.arange(s)
    w_scale = (IDX_HEADS ** -0.5) * (IDX_DIM ** -0.5)
    a_scale = A_HEAD_DIM ** -0.5
    gather = jax.vmap(lambda t, i: t[i])

    def one_block(args):
        blk, qb, iqb, iwb = args
        q_pos = blk * Q_BLOCK + jnp.arange(Q_BLOCK)
        causal = key_pos[None, :] <= q_pos[:, None]
        logits = jnp.einsum('bqhd,bsd->bqhs', iqb, ik).astype(jnp.float32)
        score = jnp.einsum('bqhs,bqh->bqs', jax.nn.relu(logits), iwb.astype(jnp.float32)) * w_scale
        score = jnp.where(causal[None], score, -jnp.inf)
        _, sel = lax.top_k(score, n_sel)
        k_sel = gather(k, sel)
        v_sel = gather(v, sel)
        valid = sel <= q_pos[None, :, None]
        sc = jnp.einsum('bqhd,bqnd->bqhn', qb, k_sel).astype(jnp.float32) * a_scale
        sc = jnp.where(valid[:, :, None, :], sc, -jnp.inf)
        p = jax.nn.softmax(sc, axis=-1).astype(v.dtype)
        return jnp.einsum('bqhn,bqnd->bqhd', p, v_sel)

    nblk = s // Q_BLOCK
    out = lax.map(one_block, (jnp.arange(nblk), to_blocks(q, Q_BLOCK),
                              to_blocks(iq, Q_BLOCK), to_blocks(iw, Q_BLOCK)))
    return from_blocks(out)

def moba_attention(q, k, v):
    b, s, h, d = q.shape
    nb = -(-s // MOBA_BLOCK)
    pad = nb * MOBA_BLOCK - s

    def blocks(a):
        a = jnp.pad(a, ((0, 0), (0, pad), (0, 0), (0, 0)))
        return a.reshape(b, nb, MOBA_BLOCK, h, d).transpose(0, 3, 1, 2, 4)

    kb = blocks(k)
    vb = blocks(v)
    k_mean = jnp.mean(kb.astype(jnp.float32), axis=3).astype(k.dtype)
    n_top = min(MOBA_TOPK, nb - 1)
    scale = d ** -0.5
    blk_ids = jnp.arange(nb)
    key_in_blk = jnp.arange(MOBA_BLOCK)
    gather = jax.vmap(jax.vmap(lambda t, i: t[i]))

    def one_chunk(args):
        c, qc = args
        q_pos = c * MOBA_Q_CHUNK + jnp.arange(MOBA_Q_CHUNK)
        own = (c * MOBA_Q_CHUNK) // MOBA_BLOCK
        k_own = lax.dynamic_index_in_dim(kb, own, axis=2, keepdims=False)
        v_own = lax.dynamic_index_in_dim(vb, own, axis=2, keepdims=False)
        s_own = jnp.einsum('bqhd,bhkd->bhqk', qc, k_own).astype(jnp.float32) * scale
        s_own = jnp.where((own * MOBA_BLOCK + key_in_blk)[None, :] <= q_pos[:, None], s_own, -jnp.inf)
        if n_top == 0:
            p = jax.nn.softmax(s_own, axis=-1).astype(v.dtype)
            return jnp.einsum('bhqk,bhkd->bqhd', p, v_own)
        gate = jnp.einsum('bqhd,bhnd->bhqn', qc, k_mean).astype(jnp.float32)
        gate = jnp.where(blk_ids < own, gate, -jnp.inf)
        _, sel = lax.top_k(gate, n_top)
        k_sel = gather(kb, sel)
        v_sel = gather(vb, sel)
        s_past = jnp.einsum('bqhd,bhqnkd->bhqnk', qc, k_sel).astype(jnp.float32) * scale
        s_past = jnp.where((sel < own)[..., None], s_past, -jnp.inf)
        s_past = s_past.reshape(b, h, MOBA_Q_CHUNK, n_top * MOBA_BLOCK)
        p = jax.nn.softmax(jnp.concatenate([s_past, s_own], axis=-1), axis=-1).astype(v.dtype)
        p_past = p[..., :n_top * MOBA_BLOCK].reshape(b, h, MOBA_Q_CHUNK, n_top, MOBA_BLOCK)
        p_own = p[..., n_top * MOBA_BLOCK:]
        return (jnp.einsum('bhqnk,bhqnkd->bqhd', p_past, v_sel)
                + jnp.einsum('bhqk,bhkd->bqhd', p_own, v_own))

    nchunk = s // MOBA_Q_CHUNK
    out = lax.map(one_chunk, (jnp.arange(nchunk), to_blocks(q, MOBA_Q_CHUNK)))
    return from_blocks(out)

def even_mixer(h, cos64, sin64, w_in, w_out):
    b, s, _ = h.shape
    qa, ka, va, iq, ik, iw, qb, kb, vb = jnp.split(h @ w_in, EVEN_SPLITS, axis=-1)
    qa = apply_rope(qa.reshape(b, s, A_HEADS, A_HEAD_DIM), cos64, sin64)
    ka = apply_rope(ka[:, :, None, :], cos64, sin64)[:, :, 0]
    iq = apply_rope(iq.reshape(b, s, IDX_HEADS, IDX_DIM), cos64, sin64)
    ik = apply_rope(ik[:, :, None, :], cos64, sin64)[:, :, 0]
    out_a = dsa_attention(qa, ka, va, iq, ik, iw)
    qb = apply_rope(qb.reshape(b, s, B_HEADS, B_HEAD_DIM), cos64, sin64)
    kb = apply_rope(kb.reshape(b, s, B_HEADS, B_HEAD_DIM), cos64, sin64)
    vb = vb.reshape(b, s, B_HEADS, B_HEAD_DIM)
    out_b = moba_attention(qb, kb, vb)
    o = jnp.concatenate([out_a.reshape(b, s, A_HEADS * A_HEAD_DIM),
                         out_b.reshape(b, s, B_HEADS * B_HEAD_DIM)], axis=-1)
    return o @ w_out

def mla_attention(q_nope, q_rope, k_nope, k_rope, v):
    s = q_nope.shape[1]
    key_pos = jnp.arange(s)
    scale = (C_NOPE + C_ROPE) ** -0.5

    def one_block(args):
        blk, qn, qr = args
        q_pos = blk * Q_BLOCK + jnp.arange(Q_BLOCK)
        sc = (jnp.einsum('bqhd,bshd->bhqs', qn, k_nope)
              + jnp.einsum('bqhd,bsd->bhqs', qr, k_rope)).astype(jnp.float32) * scale
        sc = jnp.where(key_pos[None, :] <= q_pos[:, None], sc, -jnp.inf)
        p = jax.nn.softmax(sc, axis=-1).astype(v.dtype)
        return jnp.einsum('bhqs,bshd->bqhd', p, v)

    nblk = s // Q_BLOCK
    out = lax.map(one_block, (jnp.arange(nblk), to_blocks(q_nope, Q_BLOCK), to_blocks(q_rope, Q_BLOCK)))
    return from_blocks(out)

def mla_mixer(h, cos32, sin32, w_in, q_norm, kv_norm, w_uq, w_ukv, w_out):
    b, s, _ = h.shape
    cq, ckv, kr = jnp.split(h @ w_in, [C_Q_RANK, C_Q_RANK + C_KV_RANK], axis=-1)
    q = (rms_norm_2(cq, q_norm) @ w_uq).reshape(b, s, C_HEADS, C_NOPE + C_ROPE)
    q_nope, q_rope = jnp.split(q, [C_NOPE], axis=-1)
    q_rope = apply_rope(q_rope, cos32, sin32)
    kv = (rms_norm_2(ckv, kv_norm) @ w_ukv).reshape(b, s, C_HEADS, C_NOPE + C_V)
    k_nope, v = jnp.split(kv, [C_NOPE], axis=-1)
    k_rope = apply_rope(kr[:, :, None, :], cos32, sin32)[:, :, 0]
    o = mla_attention(q_nope, q_rope, k_nope, k_rope, v)
    return o.reshape(b, s, C_HEADS * C_V) @ w_out

def peer_ffn(h, w_q, sub_keys, u_tab, v_tab):
    b, s, d = h.shape
    tokens = h.reshape(b * s // PEER_CHUNK, PEER_CHUNK, d)

    def one_chunk(xc):
        t = xc.shape[0]
        q = (xc @ w_q).reshape(t, PEER_HEADS, 2, PEER_QDIM // 2)
        sc = jnp.einsum('thpc,hpnc->thpn', q, sub_keys).astype(jnp.float32)
        v_half, i_half = lax.top_k(sc, PEER_TOPK_HALF)
        cand = (v_half[:, :, 0, :, None] + v_half[:, :, 1, None, :]).reshape(t, PEER_HEADS, -1)
        cand_idx = (i_half[:, :, 0, :, None] * PEER_NKEYS + i_half[:, :, 1, None, :]).reshape(t, PEER_HEADS, -1)
        top_s, pos = lax.top_k(cand, PEER_TOPK)
        expert = jnp.take_along_axis(cand_idx, pos, axis=-1)
        g = jax.nn.softmax(top_s, axis=-1)
        u = u_tab[expert]
        act = jax.nn.gelu(jnp.einsum('thkd,td->thk', u, xc).astype(jnp.float32), approximate=False)
        w = (g * act).astype(xc.dtype)
        return jnp.einsum('thk,thkd->td', w, v_tab[expert])

    return lax.map(one_chunk, tokens).reshape(b, s, d)

def second_inputs(seed: int = 0) -> dict:
    key = jax.random.key(seed)
    ks = jax.random.split(key, 20)
    f32 = jnp.float32

    def nrm(k, shape, scale):
        return jax.random.normal(k, shape, f32) * scale

    def gain(k, shape):
        return 1.0 + 0.02 * jax.random.normal(k, shape, f32)

    return {
        'x': jax.random.normal(ks[0], (BATCH, SEQ, D_MODEL), f32),
        'positions': jnp.broadcast_to(jnp.arange(SEQ, dtype=jnp.int32)[None, :], (BATCH, SEQ)),
        'attn_norm': gain(ks[1], (DEPTH_2, D_MODEL)),
        'ffn_norm': gain(ks[2], (DEPTH_2, D_MODEL)),
        'final_norm': gain(ks[3], (D_MODEL,)),
        'hyb_w_in': nrm(ks[4], (N_EVEN, D_MODEL, EVEN_IN_COLS), D_MODEL ** -0.5),
        'hyb_w_out': nrm(ks[5], (N_EVEN, EVEN_OUT_COLS, D_MODEL), EVEN_OUT_COLS ** -0.5),
        'mla_w_in': nrm(ks[6], (N_ODD, D_MODEL, C_IN_COLS), D_MODEL ** -0.5),
        'mla_q_norm': gain(ks[7], (N_ODD, C_Q_RANK)),
        'mla_kv_norm': gain(ks[8], (N_ODD, C_KV_RANK)),
        'mla_w_uq': nrm(ks[9], (N_ODD, C_Q_RANK, C_HEADS * (C_NOPE + C_ROPE)), C_Q_RANK ** -0.5),
        'mla_w_ukv': nrm(ks[10], (N_ODD, C_KV_RANK, C_HEADS * (C_NOPE + C_V)), C_KV_RANK ** -0.5),
        'mla_w_out': nrm(ks[11], (N_ODD, C_HEADS * C_V, D_MODEL), (C_HEADS * C_V) ** -0.5),
        'peer_w_q': nrm(ks[12], (DEPTH_2, D_MODEL, PEER_HEADS * PEER_QDIM), D_MODEL ** -0.5),
        'peer_sub_keys': nrm(ks[13], (DEPTH_2, PEER_HEADS, 2, PEER_NKEYS, PEER_QDIM // 2), (PEER_QDIM // 2) ** -0.5),
        'peer_u': nrm(ks[14], (DEPTH_2, PEER_N_EXPERTS, D_MODEL), D_MODEL ** -0.5),
        'peer_v': nrm(ks[15], (DEPTH_2, PEER_N_EXPERTS, D_MODEL), D_MODEL ** -0.5),
    }

def second_block(x, positions, attn_norm, ffn_norm, final_norm, hyb_w_in, hyb_w_out,
              mla_w_in, mla_q_norm, mla_kv_norm, mla_w_uq, mla_w_ukv, mla_w_out,
              peer_w_q, peer_sub_keys, peer_u, peer_v):
    cos64, sin64 = rope_tables(positions, A_HEAD_DIM)
    cos32, sin32 = rope_tables(positions, C_ROPE)
    for i in range(DEPTH_2):
        h = rms_norm_2(x, attn_norm[i])
        j = i // 2
        if i % 2 == 0:
            x = x + even_mixer(h, cos64, sin64, hyb_w_in[j], hyb_w_out[j])
        else:
            x = x + mla_mixer(h, cos32, sin32, mla_w_in[j], mla_q_norm[j], mla_kv_norm[j],
                              mla_w_uq[j], mla_w_ukv[j], mla_w_out[j])
        h = rms_norm_2(x, ffn_norm[i])
        x = x + peer_ffn(h, peer_w_q[i], peer_sub_keys[i], peer_u[i], peer_v[i])
    return rms_norm_2(x, final_norm)


def setup_inputs(seed=0):
    out = dict(first_inputs(seed))
    for name, value in second_inputs(seed + 1).items():
        if name != "x":
            out[name + "_2"] = value
    return out


def reference(
    x, c, positions, w_ada, b_ada, g_pre_mix, g_post_mix, g_pre_ffn, g_post_ffn, w_in, w_pool,
    b_pool, pool_scale, w_out, w_up, conv_w, conv_b, w_down, positions_2, attn_norm_2,
    ffn_norm_2, final_norm_2, hyb_w_in_2, hyb_w_out_2, mla_w_in_2, mla_q_norm_2, mla_kv_norm_2,
    mla_w_uq_2, mla_w_ukv_2, mla_w_out_2, peer_w_q_2, peer_sub_keys_2, peer_u_2, peer_v_2,
):
    x = first_block(
        x, c, positions, w_ada, b_ada, g_pre_mix, g_post_mix, g_pre_ffn, g_post_ffn, w_in,
        w_pool, b_pool, pool_scale, w_out, w_up, conv_w, conv_b, w_down,
    )
    return second_block(
        x, positions_2, attn_norm_2, ffn_norm_2, final_norm_2, hyb_w_in_2, hyb_w_out_2,
        mla_w_in_2, mla_q_norm_2, mla_kv_norm_2, mla_w_uq_2, mla_w_ukv_2, mla_w_out_2,
        peer_w_q_2, peer_sub_keys_2, peer_u_2, peer_v_2,
    )


_drawn_inputs = setup_inputs


def setup_inputs(seed=0):
    import zlib

    import numpy as np

    out = dict(_drawn_inputs(seed))
    spreads = {}
    factors = {'b_pool': 3.189,
     'conv_b': 4.742,
     'attn_norm_2': 3.709,
     'ffn_norm_2': 8.0,
     'final_norm_2': 2.838,
     'mla_q_norm_2': 8.0,
     'mla_kv_norm_2': 8.0,
     'peer_w_q_2': 3.669,
     'peer_sub_keys_2': 3.68,
     'peer_u_2': 4.106,
     'peer_v_2': 3.675}
    for name, (base, spread) in spreads.items():
        noise = np.random.default_rng([zlib.crc32(name.encode()), seed]).standard_normal(out[name].shape)
        drawn = base * np.exp(spread * noise) if base else spread * noise
        out[name] = __import__('jax').numpy.asarray(drawn.astype(out[name].dtype))
    for name, factor in factors.items():
        out[name] = (out[name] * factor).astype(out[name].dtype)
    return out
```

```python
import os
import numpy as np
import concourse.bass as bass
from concourse import mybir
from contextlib import ExitStack

F32 = mybir.dt.float32
U32 = mybir.dt.uint32
I32 = mybir.dt.int32
ALU = mybir.AluOpType
ACT = mybir.ActivationFunctionType
AX = mybir.AxisListType

D = 1024
NEG = -1.0e30
LOW = -3.0e38
EPS = 1e-6
D_FF = 2816
NGATHER = 10
NWS = 3
R1, R2, R3 = 1.2, 1.2, 1.2

C_ID, C_MASK, C_FREQ, C_SGN, C_IOTA, C_END = 0, 128, 2176, 2288, 2400, 2416


class Queue:

    def __init__(self, sem):
        self.sem, self.items, self.n, self.seen = sem, [], 0, {}

    def wait(self, *tokens):
        for t in tokens:
            if t is None:
                continue
            if isinstance(t, list):
                self.wait(*t)
                continue
            key, sem, value = t
            if self.seen.get(key, 0) < value:
                self.seen[key] = value
                self.items.append((None, sem, value))

    def __call__(self, f, *tokens, inc=True):
        self.wait(*tokens)
        if not inc:
            self.items.append((f, None, 0))
            return None
        self.n += 1
        self.items.append((f, self.sem, 1))
        return (id(self), self.sem, self.n)

    def dma(self, f, slot, *tokens):
        self.wait(*tokens)
        slot.count += 16
        self.items.append((f, slot.sem, 16))
        return (id(slot), slot.sem, slot.count)

    def emit(self, eng):
        for f, sem, value in self.items:
            if f is None:
                eng.wait_ge(sem, value)
            elif sem is None:
                f(eng)
            else:
                f(eng).then_inc(sem, value)


class Slot:

    def __init__(self, ap, sem=None):
        self.ap, self.sem, self.count, self.free = ap, sem, 0, []


class Ring:
    def __init__(self, slots):
        self.slots, self.i = slots, 0

    def take(self):
        s = self.slots[self.i % len(self.slots)]
        self.i += 1
        return s


def program(nc, a, out):
    ctx = ExitStack()
    with ctx:
        def sb(name, cols, dt=F32):
            return ctx.enter_context(nc.sbuf_tensor(name, [128, cols], dt))

        def sem(name):
            return ctx.enter_context(nc.semaphore(name))

        PS = ctx.enter_context(nc.psum_tensor("PS", [128, 4096], F32))
        consts = sb("consts", C_END)
        xs = sb("xs", 2 * D)
        hs = sb("hs", 2 * D)
        hTs = sb("hTs", 8 * 256)
        gains = sb("gains", 6 * D)
        tabs = sb("tabs", 4 * 112)
        small = sb("small", 512)
        wring = sb("wring", NWS * 4096)
        gring = sb("gring", NGATHER * D)
        keep = sb("keep", 6144)
        work = sb("work", 7232)
        diags = sb("diags", 4 * 128)
        sel_idx = sb("sel_idx", 2 * 128, U32)
        sel_g = sb("sel_g", 2 * 128)
        acts = sb("acts", 2 * 128)
        ipos = sb("ipos", 4, I32)

        V, A, T, G, S = (Queue(sem(n)) for n in ("s_v", "s_a", "s_t", "s_g", "s_s"))
        banks = Ring([Slot(PS[:, 512 * i:512 * (i + 1)]) for i in range(6)])
        ybank = [PS[:, 512 * i:512 * (i + 1)] for i in (6, 7)]
        wslots = Ring([Slot(wring[:, 4096 * i:4096 * (i + 1)], sem(f"s_w{i}")) for i in range(NWS)])
        gslots = Ring([Slot(gring[:, D * i:D * (i + 1)], sem(f"s_u{i}")) for i in range(NGATHER)])
        dslots = Ring([Slot(diags[:, 128 * i:128 * (i + 1)]) for i in range(4)])
        loads = Slot(None, sem("s_ld"))
        loads2 = Slot(None, sem("s_ld2"))
        outs = Slot(None, sem("s_out"))

        ident = consts[:, C_ID:C_ID + 128]
        mask = consts[:, C_MASK:C_MASK + 2048].rearrange("p (g t s) -> p g t s", g=4, t=2)
        iota = consts[:, C_IOTA:C_IOTA + 16]
        x = [xs[:, D * t:D * (t + 1)] for t in range(2)]
        h = [hs[:, D * t:D * (t + 1)] for t in range(2)]
        hT = hTs[:, :].rearrange("p (k s) -> p k s", k=8)
        gain = [gains[:, D * i:D * (i + 1)] for i in range(6)]
        cc = tabs[:, 0:224].rearrange("p (t c) -> p t c", t=2)
        ss = tabs[:, 224:448].rearrange("p (t c) -> p t c", t=2)
        xtok = [None, None]

        def bar():
            ends = [(id(q), q.sem, q.n) for q in (V, A, T, G) if q.n]
            for q in (V, A, T, G, S):
                q.wait(*ends)

        def bcast(ap, n):
            return ap.partition_broadcast(128)

        def load(slot, dst, src, *tok):
            return S.dma(lambda e: e.dma_start(dst, src), slot, *tok)

        consts_in = consts[:, :]
        load(loads, consts_in, a["consts"])
        load(loads, x[0], a["x"][0, 0:128, :])
        load(loads, x[1], a["x"][0, 128:256, :])
        cw = keep[:, 0:128]
        cT8 = small[:, 0:8]
        crow = keep[0:8, 128:256]
        load(loads, crow, a["c"].rearrange("o (r c) -> (o r) c", c=128))
        load(loads, cw[0:66, :], a["conv_w"][0].rearrange("t (j c) -> (t j) c", c=128))
        load(loads, cw[66:88, :], a["conv_b"].rearrange("o (j c) -> (o j) c", c=128))
        for i, n in enumerate(("g_pre_mix", "g_post_mix", "g_pre_ffn", "g_post_ffn")):
            load(loads, gain[i], a[n][0].partition_broadcast(128))
        load(loads, ipos[:, :], a["pos"])
        mod = gring[:, 0:6 * D]
        poolB = gring[:, 6 * D:8 * D].rearrange("p (s g t) -> p s g t", s=2, g=4)
        load(loads, gring[:, 6 * D:8 * D], a["pool_band"])
        load(loads, mod, a["b_ada"][0].partition_broadcast(128))
        bp = gring[:, 8 * D:8 * D + 512]
        load(loads, bp[:, 0:256], a["b_pool"][0].rearrange("g c -> (g c)").partition_broadcast(128))
        load(loads, bp[:, 256:512], a["pool_scale"][0].partition_broadcast(128))
        wp = gring[0:64, 8 * D + 512:8 * D + 768].rearrange("p (g c) -> p g c", g=4)
        ld = load(loads, wp, a["w_pool"][0].rearrange("g c d -> c g d"))
        for q in (V, A, T, G):
            q.wait(ld)

        def load_w(parts):
            s = wslots.take()
            view = s.ap.rearrange("p (k n) -> p k n", n=512)
            tok = None
            for col, w, r0, nk, c0, n in parts:
                src = w[r0:r0 + 128 * nk, c0:c0 + n].rearrange("(k p) n -> p k n", p=128)
                tok = S.dma(lambda e, d=view[:, 0:nk, col:col + n], src=src: e.dma_start(d, src), s, s.free)
            return s, view, tok

        def project(tiles, lhs, ltok, w, K, cols, evac):
            kt = K // 128
            for c0, n in cols:
                bk = {t: banks.take() for t in tiles}
                for k0 in range(0, kt, 8):
                    nk = min(8, kt - k0)
                    s, view, tok = load_w([(0, w, 128 * k0, nk, c0, n)])
                    for t in tiles:
                        for k in range(nk):
                            if k == 4:
                                yield 3.4
                            m = T(lambda e, o=bk[t].ap[:, 0:n], l=lhs(k0 + k, t), r=view[:, k, 0:n],
                                  a0=(k0 + k == 0), z=(k0 + k == kt - 1): e.matmul(o, l, r, start=a0, stop=z),
                                  tok, ltok, bk[t].free, inc=(k == nk - 1))
                        if k0 + nk == kt:
                            bk[t].done = m
                    s.free = [m]
                for t in tiles:
                    bk[t].free = evac(t, c0, n, bk[t].ap[:, 0:n], bk[t].done)
                yield 3.4

        flip = [0]

        def copy(dst, src, *tok):
            flip[0] ^= 1
            if flip[0]:
                return A(lambda e: e.activation(dst, src, ACT.Copy), *tok)
            return V(lambda e: e.tensor_copy(dst, src), *tok)

        def transposes(srcs, dst, tok, wtok=None):
            toks = []
            for i0 in range(0, len(srcs), 4):
                grp = srcs[i0:i0 + 4]
                b = banks.take()
                c = grp[0].shape[1]
                for i, s in enumerate(grp):
                    m = T(lambda e, o=b.ap[0:c, 128 * i:128 * i + 128], s=s: e.transpose(o, s, ident),
                          tok, b.free, inc=(i == len(grp) - 1))
                t = copy(dst(i0, len(grp)), b.ap[0:c, 0:128 * len(grp)].rearrange("p (b q) -> p b q", q=128), m, wtok)
                b.free = [t]
                toks.append(t)
            return toks

        nsm = [32]

        def sm(n):
            if nsm[0] + n > 512:
                nsm[0] = 32
            nsm[0] += n
            return small[:, nsm[0] - n:nsm[0]]

        def rstd(src, n, junk, *tok):
            s = sm(8)
            t = A(lambda e: e.activation(junk, src, ACT.Square, accum_out=s[:, 0:1]), *tok)
            t = V(lambda e: e.tensor_scalar(s[:, 1:2], s[:, 0:1], 1.0 / n, EPS, ALU.mult, ALU.add), t)
            t = A(lambda e: e.activation(s[:, 2:3], s[:, 1:2], ACT.Sqrt), t)
            t = V(lambda e: e.reciprocal(s[:, 3:4], s[:, 2:3]), t)
            t = V(lambda e: e.tensor_tensor(s[:, 4:5], s[:, 3:4], s[:, 3:4], ALU.mult), t)
            t = V(lambda e: e.tensor_tensor(s[:, 5:6], s[:, 4:5], s[:, 1:2], ALU.mult), t)
            t = V(lambda e: e.tensor_scalar(s[:, 6:7], s[:, 5:6], -0.5, 1.5, ALU.mult, ALU.add), t)
            t = V(lambda e: e.tensor_tensor(s[:, 7:8], s[:, 3:4], s[:, 6:7], ALU.mult), t)
            return s[:, 7:8], t

        def norm(dst, src, g, n, junk, *tok):
            r, t = rstd(src, n, junk, *tok)
            return V(lambda e: e.scalar_tensor_tensor(dst, src, r, g, ALU.mult, ALU.mult), t)

        sbuf_s = Ring([Slot(work[:, 768 * i:768 * (i + 1)]) for i in range(2)])
        sbuf_t = Ring([Slot(work[:, 1536 + 768 * i:1536 + 768 * (i + 1)]) for i in range(2)])

        def att_scores(tile, segs, scale, tok):
            nk = 128 * (tile + 1)
            n = len(segs)
            buf = sbuf_s.take()
            s = sm(8)
            tt = []
            for g, (q, k, v, m) in enumerate(segs):
                b = banks.take()
                t = T(lambda e, o=b.ap[:, 0:nk], q=q, k=k[:, 0:nk]: e.matmul(o, q, k, start=True, stop=True),
                      tok, b.free)
                t = V(lambda e, o=buf.ap[:, nk * g:nk * g + nk], i=b.ap[:, 0:nk], m=m[:, 0:nk], r=s[:, g:g + 1]:
                      e.tensor_tensor_reduce(o, i, m, 1.0, LOW, ALU.add, ALU.max, r), t, buf.free)
                b.free = [t]
            if n > 1:
                t = V(lambda e: e.tensor_reduce(s[:, 3:4], s[:, 0:n], AX.X, ALU.max), t)
                top = s[:, 3:4]
            else:
                top = s[:, 0:1]
            t = V(lambda e: e.tensor_scalar(s[:, 4:5], top, -scale, None, ALU.mult), t)
            p = buf.ap[:, 0:nk * n]
            t = A(lambda e: e.activation(p, p, ACT.Exp, bias=s[:, 4:5], scale=scale, accum_out=s[:, 5:6]), t)
            return tile, segs, buf, s, t

        def att_values(state, dst):
            tile, segs, buf, s, te = state
            nt = tile + 1
            tr = V(lambda e: e.reciprocal(s[:, 6:7], s[:, 5:6]), te)
            pt = sbuf_t.take()
            nb = nt * len(segs)
            ptv = pt.ap.rearrange("p (b q) -> p b q", q=128)
            tk = transposes([buf.ap[:, 128 * i:128 * i + 128] for i in range(nb)],
                            lambda i0, n: ptv[:, i0:i0 + n, :], te, pt.free)
            buf.free = [(id(T), T.sem, T.n)]
            b = banks.take()
            for i in range(nb):
                v = segs[i // nt][2](i % nt)
                t = T(lambda e, o=b.ap[:, 0:64], l=ptv[:, i, :], v=v, i=i: e.matmul(o, l, v, start=(i == 0),
                      stop=(i == nb - 1)), tk, b.free, inc=(i == nb - 1))
            pt.free = [t]
            t = V(lambda e, o=b.ap[:, 0:64]: e.tensor_scalar(dst, o, s[:, 6:7], None, ALU.mult), t, tr)
            b.free = [t]
            return t

        def attention(units, tok):
            prev, out_t = None, []
            for tile, segs, scale, dst in units:
                st = att_scores(tile, segs, scale, tok)
                if prev:
                    out_t = [att_values(*prev)]
                prev = (st, dst)
                yield 2.5
            out_t = [att_values(*prev)]
            attention.tok = out_t

        angb = work[:, 0:1120].rearrange("p (b t c) -> p b t c", b=5, t=2)
        t = V(lambda e: e.tensor_copy(small[:, 8:12], ipos[:, 0:4]))
        freq = consts[:, C_FREQ:C_FREQ + 112]
        sgn = consts[:, C_SGN:C_SGN + 112]
        for tl in range(2):
            V(lambda e, tl=tl: e.tensor_scalar(angb[:, 0, tl, 0:16], freq[:, 0:16], small[:, 8 + tl:9 + tl], None,
                                               ALU.mult), t)
            V(lambda e, tl=tl: e.tensor_scalar(angb[:, 0, tl, 16:112], freq[:, 16:112],
                                               small[:, 10 + tl:11 + tl], None, ALU.mult), t)
        P2 = 2.0 * np.pi
        C1 = 6.28125
        C2 = float(np.float32(np.round((P2 - C1) * 2 ** 22) / 2 ** 22))
        C3 = float(np.float32(P2 - C1 - C2))
        MG = 12582912.0
        PI = float(np.nextafter(np.float32(np.pi), np.float32(0)))
        for dstt, shift, back in ((ss, 0.0, 0.0), (cc, 0.25, float(np.float32(np.pi / 2)))):
            ang, n1, r1, r2 = (angb[:, i, :, :] for i in range(4))
            t = (id(V), V.sem, V.n)
            t = V(lambda e, shift=shift: e.tensor_scalar(n1, ang, 1.0 / P2, shift, ALU.mult, ALU.add), t)
            t = V(lambda e: e.tensor_scalar(n1, n1, MG, None, ALU.add), t)
            t = V(lambda e: e.tensor_scalar(n1, n1, -MG, None, ALU.add), t)
            t = V(lambda e: e.scalar_tensor_tensor(r1, n1, -C1, ang, ALU.mult, ALU.add), t)
            t = V(lambda e: e.scalar_tensor_tensor(r2, n1, -C2, r1, ALU.mult, ALU.add), t)
            t = V(lambda e: e.scalar_tensor_tensor(r1, n1, -C3, r2, ALU.mult, ALU.add), t)
            t = V(lambda e, back=back: e.tensor_scalar(r2, r1, back, PI, ALU.add, ALU.min), t)
            t = V(lambda e: e.tensor_scalar(r1, r2, -PI, None, ALU.max), t)
            ta = A(lambda e, dstt=dstt: e.activation(dstt, r1, ACT.Sin), t)
            V.wait(ta)
        V(lambda e: e.tensor_tensor(ss, ss, sgn.unsqueeze(1).to_broadcast([128, 2, 112]), ALU.mult), ta)
        TR16, TR64, TR32 = (0, 16), (16, 64), (80, 32)

        def rope(dst, src, tile, which, heads, b1, b2, *tok):
            o, w = which
            hw = w // 2
            c = cc[:, tile, o:o + w].unsqueeze(1).to_broadcast([128, heads, w])
            s0 = ss[:, tile, o:o + hw].unsqueeze(1).to_broadcast([128, heads, hw])
            s1 = ss[:, tile, o + hw:o + w].unsqueeze(1).to_broadcast([128, heads, hw])
            va = b1[:, 0:heads * w].rearrange("p (h w) -> p h w", w=w)
            vb = b2[:, 0:heads * w].rearrange("p (h w) -> p h w", w=w)
            V(lambda e: e.tensor_tensor(va, src, c, ALU.mult), *tok)
            V(lambda e: e.tensor_tensor(vb[:, :, 0:hw], src[:, :, hw:w], s0, ALU.mult))
            t = V(lambda e: e.tensor_tensor(vb[:, :, hw:w], src[:, :, 0:hw], s1, ALU.mult))
            return t, V(lambda e: e.tensor_tensor(dst, va, vb, ALU.add), t)

        def run(gen):
            for _ in gen:
                pass

        s = sm(32)
        b = banks.take()
        T(lambda e: e.transpose(b.ap[:, 0:8], crow, ident[0:8, 0:8]), inc=False)
        t = T(lambda e: e.transpose(b.ap[:, 128:216], cw[0:88, :], ident[0:88, 0:88]))
        cwT = keep[:, 256:344]
        V(lambda e: e.tensor_copy(cT8, b.ap[:, 0:8]), t)
        t = V(lambda e: e.tensor_copy(cwT, b.ap[:, 128:216]), t)
        b.free = [t]
        t = A(lambda e: e.activation(s[:, 0:8], cT8, ACT.Exp, scale=-1.0), t)
        t = V(lambda e: e.tensor_scalar(s[:, 8:16], s[:, 0:8], 1.0, None, ALU.add), t)
        t = V(lambda e: e.reciprocal(s[:, 16:24], s[:, 8:16]), t)
        t = V(lambda e: e.tensor_tensor(s[:, 24:32], s[:, 16:24], cT8, ALU.mult), t)
        ones = keep[:, 384:512]
        to = V(lambda e: e.memset(ones, 1.0))
        cact = s[:, 24:32]
        accs = Ring([Slot(work[:, 6144 + 512 * i:6656 + 512 * i]) for i in range(2)])

        def modulation():
            for i in range(12):
                sl, view, tok = load_w([(0, a["w_ada"][0], 0, 8, 512 * i, 512)])
                ac = accs.take()
                tv = V(lambda e, ac=ac, view=view: e.tensor_scalar(ac.ap, view[:, 0, :], cact[:, 0:1], None, ALU.mult), tok, ac.free, t)
                for k in range(1, 8):
                    tv = V(lambda e, k=k, ac=ac, view=view: e.scalar_tensor_tensor(ac.ap, view[:, k, :], cact[:, k:k + 1], ac.ap,
                                                                 ALU.mult, ALU.add), tv)
                sl.free = [tv]
                b = banks.take()
                tm = T(lambda e, b=b, ac=ac: e.matmul(b.ap, ones, ac.ap, start=True, stop=True), tv, to, b.free)
                ac.free = [tm]
                mc = mod[:, 512 * i:512 * i + 512]
                tv = V(lambda e, b=b, mc=mc: e.tensor_tensor(mc, b.ap, mc, ALU.add), tm)
                b.free = [tv]
                yield

        sh_m, sc_m, gt_m, sh_f, sc_f, gt_f = (mod[:, D * i:D * (i + 1)] for i in range(6))
        mods = modulation()
        for _ in range(4):
            next(mods)
        V(lambda e: e.scalar_tensor_tensor(sc_m, sc_m, 1.0, gain[0], ALU.add, ALU.mult), (id(V), V.sem, V.n))
        bar()

        def modulated(sc, sh):
            for tl in range(2):
                t = norm(h[tl], x[tl], sc, D, h[tl])
                t = V(lambda e, tl=tl: e.tensor_tensor(h[tl], h[tl], sh, ALU.add), t)
                transposes([h[tl][:, 128 * i:128 * i + 128] for i in range(8)],
                           lambda i0, n, tl=tl: hT[:, i0:i0 + n, 128 * tl:128 * tl + 128], t)
            bar()

        modulated(sc_m, sh_m)
        proj = keep[:, 1024:6144].rearrange("p (t c) -> p t c", t=2)

        def ev_proj(t, c0, n, ps, tok):
            return [copy(proj[:, t, c0:c0 + n], ps, tok)]

        for n, _ in enumerate(project([0, 1], lambda k, t: hT[:, k, 128 * t:128 * t + 128], None, a["w_in"][0], D,
                                      [(512 * i, 512) for i in range(5)], ev_proj)):
            if n % 3 == 2:
                next(mods)
        bar()
        for tl in range(2):
            src = proj[:, tl, 256:1792].rearrange("p (h w) -> p h w", w=64)[:, :, 0:16]
            rope(src, src, tl, TR16, 24, work[:, 0:384], work[:, 384:768])
            V.wait((id(V), V.sem, V.n))
        bar()
        qkT = work[:, 3072:6144].rearrange("p (b s) -> p b s", b=12)
        for tl in range(2):
            transposes([proj[:, tl, 256 + 128 * i:384 + 128 * i] for i in range(12)],
                       lambda i0, n, tl=tl: qkT[:, i0:i0 + n, 128 * tl:128 * tl + 128], None)
        bar()
        cat = hs[:, 0:1024].rearrange("p (t c) -> p t c", t=2)
        mixT = hs[0:64, 1024:2048].rearrange("p (g t) -> p g t", g=4)
        units = []
        for tl in range(2):
            for hh in range(4):
                segs = []
                for g in range(3):
                    hd = 4 * g + hh
                    r = 64 * (hd % 2)
                    segs.append((qkT[r:r + 64, hd // 2, 128 * tl:128 * tl + 128], qkT[r:r + 64, 6 + hd // 2, :],
                                 (lambda kt, hd=hd: proj[:, kt, 1792 + 64 * hd:1856 + 64 * hd]), mask[:, g, tl, :]))
                units.append((tl, segs, 0.125, cat[:, tl, 256 + 64 * hh:320 + 64 * hh]))
        for _ in attention(units, None):
            next(mods, None)
        run(mods)
        V(lambda e: e.scalar_tensor_tensor(sc_f, sc_f, 1.0, gain[2], ALU.add, ALU.mult), (id(V), V.sem, V.n))
        V(lambda e: e.tensor_tensor(gt_m, gt_m, gain[1], ALU.mult))
        V(lambda e: e.tensor_tensor(gt_f, gt_f, gain[3], ALU.mult))
        for g in range(4):
            b = banks.take()
            for si in range(2):
                t = T(lambda e, g=g, si=si, b=b: e.matmul(b.ap[0:64, 0:256], proj[:, si, 64 * g:64 * g + 64],
                      poolB[:, si, g, :], start=(si == 0), stop=(si == 1)), b.free, inc=(si == 1))
            t = copy(mixT[:, g, :], b.ap[0:64, 0:256], t)
            b.free = [t]
            T.wait(t)
        for tl in range(2):
            b = banks.take()
            for g in range(4):
                t = T(lambda e, g=g, tl=tl, b=b: e.matmul(b.ap[:, 64 * g:64 * g + 64],
                      mixT[:, g, 128 * tl:128 * tl + 128], wp[:, g, :], start=True, stop=True), b.free, inc=(g == 3))
            t = V(lambda e, tl=tl, b=b: e.tensor_tensor(cat[:, tl, 0:256], b.ap[:, 0:256], bp[:, 0:256], ALU.add), t)
            b.free = [t]
            V(lambda e, tl=tl: e.tensor_tensor(cat[:, tl, 0:256], cat[:, tl, 0:256], bp[:, 256:512], ALU.mult), t)
        bar()
        for tl in range(2):
            transposes([cat[:, tl, 128 * i:128 * i + 128] for i in range(4)],
                       lambda i0, n, tl=tl: hT[:, i0:i0 + n, 128 * tl:128 * tl + 128], None)
        bar()
        ybuf = work[:, 3072:5120].rearrange("p (t c) -> p t c", t=2)

        def ev_y(t, c0, n, ps, tok):
            return [copy(ybuf[:, t, c0:c0 + n], ps, tok)]

        run(project([0, 1], lambda k, t: hT[:, k, 128 * t:128 * t + 128], None, a["w_out"][0], 512,
                    [(0, 512), (512, 512)], ev_y))
        bar()
        junk = work[:, 0:D]

        def residual(gt):
            for tl in range(2):
                y = ybuf[:, tl, :]
                t = norm(y, y, gt, D, junk)
                V(lambda e, tl=tl, y=y: e.tensor_tensor(x[tl], x[tl], y, ALU.add), t)
                A.wait(t)
            bar()

        residual(gt_m)
        modulated(sc_f, sh_f)
        gT = keep[:, 512:512 + 22 * 256].rearrange("p (j s) -> p j s", j=22)
        cbuf = Ring([Slot(work[:, 1024 + 512 * i:1024 + 512 * (i + 1)]) for i in range(4)])
        for ch in range(11):
            sl, view, tok = load_w([(0, a["w_up"][0], 0, 8, 256 * ch, 256),
                                    (256, a["w_up"][0], 0, 8, D_FF + 256 * ch, 256)])
            bg, bv = banks.take(), banks.take()
            for b, off in ((bg, 0), (bv, 256)):
                for j in range(2):
                    for k in range(8):
                        m = T(lambda e, b=b, j=j, k=k, off=off, view=view: e.matmul(
                            b.ap[:, 256 * j:256 * j + 256], view[:, k, off + 128 * j:off + 128 * j + 128], hT[:, k, :],
                            start=(k == 0), stop=(k == 7)), tok, b.free, inc=(k == 7 and j == 1))
                b.done = m
            sl.free = [m]
            cs = cbuf.take()
            for j in range(2):
                jj = 2 * ch + j
                acc = cs.ap[:, 256 * j:256 * j + 256]
                gp = bg.ap[:, 256 * j:256 * j + 256]
                t = V(lambda e, acc=acc, gp=gp, jj=jj: e.tensor_scalar(acc, gp, cwT[:, 44 + jj:45 + jj],
                      cwT[:, 66 + jj:67 + jj], ALU.mult, ALU.add), bg.done, cs.free)
                t = V(lambda e, acc=acc, gp=gp, jj=jj: e.scalar_tensor_tensor(acc[:, 1:256], gp[:, 0:255],
                      cwT[:, 22 + jj:23 + jj], acc[:, 1:256], ALU.mult, ALU.add), t)
                t = V(lambda e, acc=acc, gp=gp, jj=jj: e.scalar_tensor_tensor(acc[:, 2:256], gp[:, 0:254],
                      cwT[:, jj:jj + 1], acc[:, 2:256], ALU.mult, ALU.add), t)
            bg.free = [t]
            t = A(lambda e, cs=cs: e.activation(cs.ap, cs.ap, ACT.Gelu_apprx_tanh), t)
            t = V(lambda e, cs=cs, bv=bv, ch=ch: e.tensor_tensor(gT[:, 2 * ch:2 * ch + 2, :],
                  cs.ap.rearrange("p (j s) -> p j s", j=2), bv.ap.rearrange("p (j s) -> p j s", j=2), ALU.mult),
                  t, bv.done)
            bv.free = [t]
            cs.free = [t]
        T.wait(t)
        run(project([0, 1], lambda k, t: gT[:, k, 128 * t:128 * t + 128], None, a["w_down"][0], D_FF,
                    [(0, 512), (512, 512)], ev_y))
        bar()
        for i, (n, r) in enumerate((("attn_norm_2", 0), ("ffn_norm_2", 0), ("attn_norm_2", 1), ("ffn_norm_2", 1))):
            load(loads2, gain[i], a[n][r].partition_broadcast(128))
        load(loads2, gain[4], a["final_norm_2"].partition_broadcast(128))
        load(loads2, gain[5][:, 0:768], a["mla_q_norm_2"][0].partition_broadcast(128))
        ldg = load(loads2, gain[5][:, 768:1024], a["mla_kv_norm_2"][0].partition_broadcast(128))
        residual(gt_f)
        V.wait(ldg)

        lhsD = lambda k, t: hT[:, k, 0:128]

        def dense_bar():
            ends = [(id(q), q.sem, q.n) for q in (V, A, T)]
            for q in (V, A, T):
                q.wait(*ends)

        def to_hT(src, nb, tok, at=0):
            return transposes([src[:, 128 * i:128 * i + 128] for i in range(nb)],
                              lambda i0, n: hT[:, at + i0:at + i0 + n, 0:128], tok)

        def add_x(tile):
            def ev(t, c0, n, ps, tok):
                xt = x[tile][:, c0:c0 + n]
                return [V(lambda e: e.tensor_tensor(xt, ps, xt, ALU.add), tok)]
            return ev

        kT6 = keep[:, 0:1536].rearrange("p (b s) -> p b s", b=6)
        vals = keep[:, 1536:2688].rearrange("p (t c) -> p t c", t=2)
        HY = [(0, 512), (512, 128), (640, 512), (1152, 72), (1224, 512), (1736, 512), (2248, 512)]

        def hybrid(tile):
            t = norm(h[tile], x[tile], gain[0], D, h[tile], xtok[tile])
            to_hT(h[tile], 8, t)
            dense_bar()
            pj = work[:, 3072:5632]
            rb = Ring([Slot(work[:, 512 * i:512 * i + 1024 - 512]) for i in range(6)])
            iw = sm(8)

            def ev(t, c0, n, ps, tok):
                spots = {0: (0, 512), 512: (1536, 64), 640: (512, 512), 1152: (1664, 64), 1224: (1024, 512),
                         1736: (1792, 512)}
                rd = []
                if c0 == 2248:
                    return [copy(vals[:, tile, 64:576], ps, tok)]
                at, w = spots[c0]
                r1, r2 = rb.take(), rb.take()
                hd = w // 64
                t3, t4 = rope(pj[:, at:at + w].rearrange("p (h w) -> p h w", w=64),
                              ps[:, 0:w].rearrange("p (h w) -> p h w", w=64), tile, TR64, hd, r1.ap, r2.ap, tok)
                rd.append(t3)
                if c0 in (512, 1152):
                    V(lambda e: e.tensor_copy(pj[:, at + 64:at + 128], pj[:, at:at + 64]), t4)
                if c0 == 512:
                    rd.append(copy(vals[:, tile, 0:64], ps[:, 64:128], t3))
                if c0 == 1152:
                    rd.append(copy(iw, ps[:, 64:72], t3))
                return rd

            yield from project([tile], lhsD, None, a["hyb_w_in_2"][0], D, HY, ev)
            dense_bar()
            qT = hTs[:, 0:1536].rearrange("p (b s) -> p b s", b=12)
            sl = slice(128 * tile, 128 * tile + 128)
            transposes([pj[:, 128 * i:128 * i + 128] for i in range(12)], lambda i0, n: qT[:, i0:i0 + n, :], None)
            transposes([pj[:, 1536 + 128 * i:1664 + 128 * i] for i in range(6)],
                       lambda i0, n: kT6[:, i0:i0 + n, sl], None)
            dense_bar()
            yield
            nk = 128 * (tile + 1)
            score = work[:, 3072:3072 + nk]
            sel = work[:, 3328:3328 + nk]
            rl = Ring([Slot(work[:, 3584 + 256 * i:3584 + 256 * i + nk]) for i in range(2)])
            for g in range(8):
                r = 64 * (g % 2)
                b = banks.take()
                t = T(lambda e, b=b, g=g, r=r: e.matmul(b.ap[:, 0:nk], qT[r:r + 64, 4 + g // 2, :],
                      kT6[r:r + 64, 1, 0:nk], start=True, stop=True), b.free)
                q = rl.take()
                t = A(lambda e, b=b, q=q: e.activation(q.ap, b.ap[:, 0:nk], ACT.Relu), t, q.free)
                b.free = [t]
                if g == 0:
                    t = V(lambda e, q=q: e.tensor_scalar(score, q.ap, iw[:, 0:1], None, ALU.mult), t)
                else:
                    t = V(lambda e, q=q, g=g: e.scalar_tensor_tensor(score, q.ap, iw[:, g:g + 1], score, ALU.mult,
                                                                     ALU.add), t, tv)
                tv = t
                q.free = [t]
            wsc = float(np.float32(8 ** -0.5 * 64 ** -0.5))
            t = V(lambda e: e.scalar_tensor_tensor(score, score, wsc, mask[:, 3, tile, 0:nk], ALU.mult, ALU.add), t)
            yield
            for i in range(8):
                m8 = sm(8)
                t = V(lambda e, m8=m8: e.max(m8, score), t)
                t = V(lambda e, m8=m8: e.match_replace(score, m8, score, LOW), t)
            t = V(lambda e: e.tensor_scalar(sel, score, LOW, 1.0, ALU.is_equal, ALU.subtract), t)
            t = V(lambda e: e.tensor_scalar(sel, sel, 1.0e30, None, ALU.mult), t)
            tsel = V(lambda e: e.tensor_tensor(sel, sel, mask[:, 3, tile, 0:nk], ALU.add), t)
            ob = work[:, 4608:5632]
            units = []
            for g in range(8):
                r = 64 * (g % 2)
                units.append((tile, [(qT[r:r + 64, 8 + g // 2, :], kT6[r:r + 64, 2 + g // 2, :],
                              (lambda kt, g=g: vals[:, kt, 64 + 64 * g:128 + 64 * g]), mask[:, 3, tile, :])], 0.125,
                             ob[:, 512 + 64 * g:576 + 64 * g]))
            for g in range(8):
                r = 64 * (g % 2)
                units.append((tile, [(qT[r:r + 64, g // 2, :], kT6[r:r + 64, 0, :],
                              (lambda kt: vals[:, kt, 0:64]), sel)], 0.125, ob[:, 64 * g:64 * g + 64]))
            V.wait(tsel)
            yield from attention(units, None)
            dense_bar()
            to_hT(ob, 8, None)
            dense_bar()
            yield from project([tile], lhsD, None, a["hyb_w_out_2"][0], D, [(0, 512), (512, 512)], add_x(tile))
            dense_bar()

        mkT = keep[:, 0:4096].rearrange("p (b s) -> p b s", b=16)
        mv = keep[:, 4096:6144].rearrange("p (t c) -> p t c", t=2)

        def mla(tile):
            sl = slice(128 * tile, 128 * tile + 128)
            t = norm(h[tile], x[tile], gain[2], D, h[tile], xtok[tile])
            to_hT(h[tile], 8, t)
            dense_bar()
            lin = work[:, 6144:7200]

            def ev(t, c0, n, ps, tok):
                return [copy(lin[:, c0:c0 + n], ps, tok)]

            yield from project([tile], lhsD, None, a["mla_w_in_2"][0], D, [(0, 512), (512, 512), (1024, 32)], ev)
            dense_bar()
            t1 = norm(lin[:, 0:768], lin[:, 0:768], gain[5][:, 0:768], 768, h[tile][:, 0:768])
            t2 = norm(lin[:, 768:1024], lin[:, 768:1024], gain[5][:, 768:1024], 256, h[tile][:, 768:1024])
            krt = work[:, 7200:7232]
            kr = lin[:, 1024:1056].unsqueeze(1)
            rope(krt.unsqueeze(1), kr, tile, TR32, 1, h[tile][:, 0:32], h[tile][:, 32:64], t2)
            to_hT(lin, 8, t2)
            dense_bar()
            qf = work[:, 3072:4608]
            kf = work[:, 4608:6144].rearrange("p (h w) -> p h w", w=96)

            def ev_q(t, c0, n, ps, tok):
                return [copy(qf[:, c0:c0 + n], ps, tok)]

            def ev_kv(t, c0, n, ps, tok):
                i = c0 // 128
                v = ps.rearrange("p (h w) -> p h w", w=128)
                t1 = copy(kf[:, i:i + 4, 0:64], v[:, :, 0:64], tok)
                return [copy(mv[:, tile, 64 * i:64 * i + 256].rearrange("p (h w) -> p h w", w=64), v[:, :, 64:128],
                             t1)]

            yield from project([tile], lhsD, None, a["mla_w_uq_2"][0], 768, [(512 * i, 512) for i in range(3)], ev_q)
            yield from project([tile], lambda k, t: hT[:, 6 + k, 0:128], None, a["mla_w_ukv_2"][0], 256,
                               [(512 * i, 512) for i in range(4)], ev_kv)
            dense_bar()
            qv = qf.rearrange("p (h w) -> p h w", w=96)[:, :, 64:96]
            rope(qv, qv, tile, TR32, 16, h[tile][:, 0:512], h[tile][:, 512:1024])
            V(lambda e: e.tensor_copy(kf[:, :, 64:96], krt.unsqueeze(1).to_broadcast([128, 16, 32])))
            dense_bar()
            qT = hTs[0:96, :].rearrange("p (b s) -> p b s", b=16)
            transposes([qf[:, 96 * i:96 * i + 96] for i in range(16)], lambda i0, n: qT[:, i0:i0 + n, :], None)
            transposes([kf[:, i, :] for i in range(16)], lambda i0, n: mkT[0:96, i0:i0 + n, sl], None)
            dense_bar()
            yield
            ob = work[:, 3072:4096]
            units = [(tile, [(qT[:, g, :], mkT[0:96, g, :], (lambda kt, g=g: mv[:, kt, 64 * g:64 * g + 64]),
                      mask[:, 3, tile, :])], float(np.float32(96 ** -0.5)), ob[:, 64 * g:64 * g + 64])
                     for g in range(16)]
            yield from attention(units, None)
            dense_bar()
            to_hT(ob, 8, None)
            dense_bar()
            yield from project([tile], lhsD, None, a["mla_w_out_2"][0], D, [(0, 512), (512, 512)], add_x(tile))
            dense_bar()

        utab = a["peer_u_2"].rearrange("l n d -> (l n) d")
        vtab = a["peer_v_2"].rearrange("l n d -> (l n) d")

        def choose(tile, l):
            t = norm(h[tile], x[tile], gain[1 + 2 * l], D, h[tile])
            to_hT(h[tile], 8, t)
            dense_bar()
            kyT = work[:, 0:2048].rearrange("p (b n) -> p b n", b=16)
            qT = work[:, 2048:4096].rearrange("p (b n) -> p b n", b=16)
            qc = Ring([Slot(work[:, 4096 + 512 * i:4096 + 512 * (i + 1)]) for i in range(2)])
            s = wslots.take()
            kv = s.ap[:, 0:2048].rearrange("p (b c) -> p b c", b=16)
            src = a["peer_sub_keys_2"][l].rearrange("h t n c -> n (h t) c")
            tk = S.dma(lambda e: e.dma_start(kv, src), s, s.free)
            transposes([kv[:, i, :] for i in range(16)], lambda i0, n: kyT[:, i0:i0 + n, :], tk)
            s.free = [(id(T), T.sem, T.n)]

            def ev(t, c0, n, ps, tok):
                q = qc.take()
                tc = copy(q.ap, ps, tok, q.free)
                i = c0 // 128
                transposes([q.ap[:, 128 * j:128 * j + 128] for j in range(4)],
                           lambda i0, n: qT[:, i + i0:i + i0 + n, :], tc)
                q.free = [(id(T), T.sem, T.n)]
                return [tc]

            yield from project([tile], lhsD, None, a["peer_w_q_2"][l], D, [(512 * i, 512) for i in range(4)], ev)
            dense_bar()
            tv = work[:, 4096:4352].rearrange("p (b k) -> p b k", k=16)
            ti = work[:, 4352:4608].bitcast(U32).rearrange("p (b k) -> p b k", k=16)
            tf = work[:, 4608:4864]
            tmp = work[:, 5120:7168].rearrange("p (b n) -> p b n", b=16)
            for g in range(4):
                b = banks.take()
                for j in range(4):
                    i = 4 * g + j
                    t = T(lambda e, b=b, i=i, j=j: e.matmul(b.ap[:, 128 * j:128 * j + 128], qT[:, i, :],
                          kyT[:, i, :], start=True, stop=True), b.free, inc=(j == 3))
                sc = [b.ap[:, 128 * j:128 * j + 128] for j in range(4)]
                ks = [4 * g + j for j in range(4)]
                t1 = [V(lambda e, i=i, s=s: e.max(tv[:, i, 0:8], s), t) for i, s in zip(ks, sc)]
                for n, (i, s) in enumerate(zip(ks, sc)):
                    V(lambda e, i=i, s=s: e.max_index(ti[:, i, 0:8], tv[:, i, 0:8], s), t1[n])
                t2 = [V(lambda e, i=i, s=s: e.match_replace(tmp[:, i, :], tv[:, i, 0:8], s, LOW))
                      for i, s in zip(ks, sc)]
                b.free = [t2[-1]]
                t3 = [V(lambda e, i=i: e.max(tv[:, i, 8:16], tmp[:, i, :]), t2[n]) for n, i in enumerate(ks)]
                for n, i in enumerate(ks):
                    V(lambda e, i=i: e.max_index(ti[:, i, 8:16], tv[:, i, 8:16], tmp[:, i, :]), t3[n])
                yield 5.0
            dense_bar()
            cand = work[:, 0:2048].rearrange("p (h i j) -> p h i j", h=8, i=16)
            cflat = work[:, 0:2048].rearrange("p (h c) -> p h c", h=8)
            tvh = work[:, 4096:4352].rearrange("p (h t k) -> p h t k", h=8, t=2)
            tfh = tf.rearrange("p (h t k) -> p h t k", h=8, t=2)
            V(lambda e: e.tensor_copy(tf, work[:, 4352:4608].bitcast(U32)))
            t = V(lambda e: e.tensor_tensor(cand, tvh[:, :, 0, :].unsqueeze(3).to_broadcast([128, 8, 16, 16]),
                  tvh[:, :, 1, :].unsqueeze(2).to_broadcast([128, 8, 16, 16]), ALU.add))
            top = work[:, 4864:4992].rearrange("p (h k) -> p h k", h=8)
            pos = work[:, 4992:5120].bitcast(U32)
            posh = pos.rearrange("p (h k) -> p h k", h=8)
            ct = work[:, 5120:7168].rearrange("p (h c) -> p h c", h=8)
            t1 = [V(lambda e, i=i: e.max(top[:, i, 0:8], cflat[:, i, :]), t) for i in range(8)]
            for i in range(8):
                V(lambda e, i=i: e.max_index(posh[:, i, 0:8], top[:, i, 0:8], cflat[:, i, :]), t1[i])
            t2 = [V(lambda e, i=i: e.match_replace(ct[:, i, :], top[:, i, 0:8], cflat[:, i, :], LOW))
                  for i in range(8)]
            t3 = [V(lambda e, i=i: e.max(top[:, i, 8:16], ct[:, i, :]), t2[i]) for i in range(8)]
            for i in range(8):
                t = V(lambda e, i=i: e.max_index(posh[:, i, 8:16], top[:, i, 8:16], ct[:, i, :]), t3[i])
            yield 12.0
            pp = work[:, 2048:2304].bitcast(U32)
            pf = work[:, 2304:2560]
            ee = work[:, 2560:2816]
            V(lambda e: e.tensor_scalar(pp[:, 0:128], pos, 4, None, ALU.logical_shift_right), t)
            t = V(lambda e: e.tensor_scalar(pp[:, 128:256], pos, 15, None, ALU.bitwise_and))
            t = V(lambda e: e.tensor_copy(pf, pp), t)
            eq = work[:, 5120:7168].rearrange("p (n i) -> p n i", i=16)
            eqh = work[:, 5120:7168].rearrange("p (h k i) -> p h k i", h=8, i=16)
            for s_ in range(2):
                t = V(lambda e, s_=s_: e.tensor_tensor(eq, pf[:, 128 * s_:128 * s_ + 128].unsqueeze(2).to_broadcast(
                    [128, 128, 16]), iota.unsqueeze(1).to_broadcast([128, 128, 16]), ALU.is_equal), t)
                t = V(lambda e, s_=s_: e.tensor_tensor(eqh, eqh, tfh[:, :, s_, :].unsqueeze(2).to_broadcast(
                    [128, 8, 16, 16]), ALU.mult), t)
                t = V(lambda e, s_=s_: e.tensor_reduce(ee[:, 128 * s_:128 * s_ + 128], eq, AX.X, ALU.add), t)
            ef = work[:, 2816:2944]
            t = V(lambda e: e.scalar_tensor_tensor(ef, ee[:, 0:128], 128.0, ee[:, 128:256], ALU.mult, ALU.add), t)
            if l:
                t = V(lambda e: e.tensor_scalar(ef, ef, float(16384 * l), None, ALU.add), t)
            ti_ = V(lambda e: e.tensor_copy(sel_idx[:, 128 * tile:128 * tile + 128], ef), t)
            ga = sel_g[:, 128 * tile:128 * tile + 128].rearrange("p (h k) -> p h k", h=8)
            s8 = sm(16)
            t = V(lambda e: e.tensor_tensor(ga, top, top[:, :, 0:1].to_broadcast([128, 8, 16]), ALU.subtract))
            t = A(lambda e: e.activation(ga, ga, ACT.Exp), t)
            t = V(lambda e: e.tensor_reduce(s8[:, 0:8], ga, AX.X, ALU.add), t)
            t = V(lambda e: e.reciprocal(s8[:, 8:16], s8[:, 0:8]), t)
            V(lambda e: e.tensor_tensor(ga, ga, s8[:, 8:16].unsqueeze(2).to_broadcast([128, 8, 16]), ALU.mult), t)
            dense_bar()
            chosen[tile] = ti_

        chosen = [None, None]
        yfree = [None]

        def gather(table, idx, tok):
            s = gslots.take()
            t = G.dma(lambda e: e.indirect_dma_start(out=s.ap, out_offset=None, in_=table,
                      in_offset=bass.IndirectOffsetOnAxis(ap=idx, axis=0)), s, s.free, tok)
            return s, t

        def experts(tile):
            tg = chosen[tile]
            tw = None
            for hd in range(9):
                c0 = 128 * tile + 16 * hd
                for j in range(16):
                    if hd < 8:
                        s, t = gather(utab, sel_idx[:, c0 + j:c0 + j + 1], tg)
                        tu = V(lambda e, s=s, c=c0 + j: e.tensor_tensor_reduce(s.ap, s.ap, h[tile], 1.0, 0.0,
                               ALU.mult, ALU.add, acts[:, c:c + 1]), t)
                        s.free = [tu]
                        yield
                    if hd:
                        c = c0 - 16 + j
                        s, t = gather(vtab, sel_idx[:, c:c + 1], tg)
                        d = dslots.take()
                        td = A(lambda e, d=d, c=c: e.activation(d.ap, ident, ACT.Copy, scale=acts[:, c:c + 1]),
                               tw, d.free)
                        st, sp = (hd == 1 and j == 0), (hd == 8 and j == 15)
                        for n in range(2):
                            m = T(lambda e, d=d, s=s, n=n, st=st, sp=sp: e.matmul(ybank[n], d.ap,
                                  s.ap[:, 512 * n:512 * n + 512], start=st, stop=sp), td, t, yfree[0], inc=(n == 1))
                        d.free = [m]
                        s.free = [m]
                        yield
                if hd < 8:
                    t = A(lambda e, c0=c0: e.activation(acts[:, c0:c0 + 16], acts[:, c0:c0 + 16], ACT.Gelu), tu)
                    tw = V(lambda e, c0=c0: e.tensor_tensor(acts[:, c0:c0 + 16], acts[:, c0:c0 + 16],
                           sel_g[:, c0:c0 + 16], ALU.mult), t)
            for n in range(2):
                t = V(lambda e, n=n: e.tensor_tensor(x[tile][:, 512 * n:512 * n + 512], ybank[n],
                      x[tile][:, 512 * n:512 * n + 512], ALU.add), m)
            yfree[0] = t
            xtok[tile] = t

        def final(tile):
            t = norm(h[tile], x[tile], gain[4], D, h[tile], xtok[tile])
            load(outs, out[0, 128 * tile:128 * tile + 128, :], h[tile], t)

        def dense(*gens):
            for g in gens:
                yield from g

        def together(fast, slow, rate):
            owed = 0.0
            done = 0
            for work_ in slow:
                owed += (work_ or 1.0) * rate
                while owed >= 1.0 and next(fast, "end") != "end":
                    owed -= 1.0
                    done += 1
            left = sum(1 for _ in fast)
            if os.environ.get("SHOW"):
                print("steps beside", done, "after", left)

        run(dense(hybrid(0), choose(0, 0)))
        together(experts(0), dense(hybrid(1), choose(1, 0)), R1)
        together(experts(1), dense(mla(0), choose(0, 1)), R2)
        together(experts(0), dense(mla(1), choose(1, 1)), R3)
        final(0)
        run(experts(1))
        final(1)
        S.wait((id(outs), outs.sem, outs.count))

        block = ctx.enter_context(nc.Block())

        @block.sync
        def _(eng):
            S.emit(eng)

        @block.vector
        def _(eng):
            V.emit(eng)

        @block.scalar
        def _(eng):
            A.emit(eng)

        @block.tensor
        def _(eng):
            T.emit(eng)

        @block.gpsimd
        def _(eng):
            G.emit(eng)


def shape_constants():
    c = np.zeros((128, C_END), np.float32)
    c[:, C_ID:C_ID + 128] = np.eye(128, dtype=np.float32)
    t = (128 * np.arange(2)[None, :, None] + np.arange(128)[:, None, None])
    s = np.arange(256)[None, None, :]
    d = t - s
    m = np.zeros((128, 4, 2, 256), np.float32)
    for g, ok in enumerate(((d >= 0) & (d <= 128), (d >= 0) & (d % 4 == 0), (d >= 0) & (d % 16 == 0), d >= 0)):
        m[:, g] = np.where(ok, 0.0, NEG)
    c[:, C_MASK:C_MASK + 2048] = m.reshape(128, 2048)
    f8 = np.float32(500000.0) ** (-np.arange(0, 16, 2, dtype=np.float32) / np.float32(16))
    f32_ = np.float32(1) / (np.float32(10000.0) ** (np.arange(0, 64, 2, dtype=np.float32) / np.float32(64)))
    f16 = np.float32(1) / (np.float32(10000.0) ** (np.arange(0, 32, 2, dtype=np.float32) / np.float32(32)))
    c[:, C_FREQ:C_FREQ + 112] = np.concatenate([f8, f8, f32_, f32_, f16, f16])
    c[:, C_SGN:C_SGN + 112] = np.concatenate([v * np.ones(n) for n in (8, 32, 16) for v in (-1, 1)])
    c[:, C_IOTA:C_IOTA + 16] = np.arange(16)
    tt, sx = np.arange(256)[None, :], np.arange(256)[:, None]
    band = np.zeros((256, 4, 256), np.float32)
    for g, w in enumerate((2, 4, 8, 16)):
        inside = (sx <= tt) & (sx > tt - w)
        band[:, g] = inside / np.minimum(tt + 1, w) - (sx == tt)
    band = band.reshape(2, 128, 4, 256).transpose(1, 0, 2, 3).reshape(128, 2048)
    return {"consts": c, "pool_band": np.ascontiguousarray(band)}


_INS = ["x", "c", "positions", "w_ada", "b_ada", "g_pre_mix", "g_post_mix", "g_pre_ffn", "g_post_ffn", "w_in",
        "w_pool", "b_pool", "pool_scale", "w_out", "w_up", "conv_w", "conv_b", "w_down", "positions_2",
        "attn_norm_2", "ffn_norm_2", "final_norm_2", "hyb_w_in_2", "hyb_w_out_2", "mla_w_in_2", "mla_q_norm_2",
        "mla_kv_norm_2", "mla_w_uq_2", "mla_w_ukv_2", "mla_w_out_2", "peer_w_q_2", "peer_sub_keys_2", "peer_u_2",
        "peer_v_2"]


def kernel(**inputs):
    import concourse.bacc as _bacc
    from concourse import mybir as _mybir
    from concourse.bass_utils import run_bass_kernel_spmd as _run

    nc = _bacc.Bacc("TRN2", target_bir_lowering=False, num_devices=1)
    arrays, args = {}, {}
    given = {n: inputs[n] for n in _INS if n[:9] != "positions"}
    given["pos"] = np.concatenate([np.asarray(inputs[n]).reshape(2, 128).T for n in ("positions", "positions_2")], 1)
    given.update(shape_constants())
    for name, value in given.items():
        v = np.ascontiguousarray(value)
        arrays[f"in_{name}_dram"] = v
        args[name] = nc.dram_tensor(f"in_{name}_dram", v.shape, _mybir.dt.from_np(v.dtype),
                                    kind="ExternalInput").ap()
    out = nc.dram_tensor("out_0_dram", (1, 256, 1024), _mybir.dt.float32, kind="ExternalOutput").ap()
    program(nc, args, out)
    r = _run(nc, [arrays], core_ids=[0])
    return r.results[0]["out_0_dram"]
```

```python
import numpy as np
import concourse.bass as bass
from concourse import mybir
from contextlib import ExitStack
from itertools import chain

F32 = mybir.dt.float32
U32 = mybir.dt.uint32
I32 = mybir.dt.int32
ALU = mybir.AluOpType
ACT = mybir.ActivationFunctionType
AX = mybir.AxisListType

D = 1024
NEG = -1.0e30
LOW = -3.0e38
EPS = 1e-6
D_FF = 2816
NGATHER = 10
NWS = 6
W = (296.0, 216.3, 243.3)

C_ID, C_MASK, C_FREQ, C_SGN, C_IOTA, C_END = 0, 128, 2176, 2288, 2400, 2416


class Queue:

    def __init__(self, sem):
        self.sem, self.items, self.n, self.seen, self.mark = sem, [], 0, {}, 0

    def wait(self, *tokens):
        for t in tokens:
            if t is None:
                continue
            if isinstance(t, list):
                self.wait(*t)
                continue
            key, sem, value = t
            if self.seen.get(key, 0) < value:
                self.seen[key] = value
                self.items.append((None, sem, value))

    def __call__(self, f, *tokens, inc=True, beside=False):
        self.wait(*tokens)
        if not inc:
            self.items.append((f, None, 0))
            return None
        self.n += 1
        if not beside:
            self.mark = self.n
        self.items.append((f, self.sem, 1))
        return (id(self), self.sem, self.n)

    def dma(self, f, slot, *tokens):
        self.wait(*tokens)
        slot.count += 16
        self.items.append((f, slot.sem, 16))
        return (id(slot), slot.sem, slot.count)

    def emit(self, eng):
        for f, sem, value in self.items:
            if f is None:
                eng.wait_ge(sem, value)
            elif sem is None:
                f(eng)
            else:
                f(eng).then_inc(sem, value)


class Slot:

    def __init__(self, ap, sem=None):
        self.ap, self.sem, self.count, self.free = ap, sem, 0, []


class Ring:
    def __init__(self, slots):
        self.slots, self.i = slots, 0

    def take(self):
        s = self.slots[self.i % len(self.slots)]
        self.i += 1
        return s


def program(nc, a, out):
    ctx = ExitStack()
    with ctx:
        def sb(name, cols, dt=F32):
            return ctx.enter_context(nc.sbuf_tensor(name, [128, cols], dt))

        def sem(name):
            return ctx.enter_context(nc.semaphore(name))

        PS = ctx.enter_context(nc.psum_tensor("PS", [128, 4096], F32))
        consts = sb("consts", C_END)
        xs = sb("xs", 2 * D)
        hs = sb("hs", 2 * D)
        hTs = sb("hTs", 8 * 256)
        gains = sb("gains", 6 * D)
        tabs = sb("tabs", 4 * 112)
        small = sb("small", 512)
        wring = sb("wring", NWS * 2048)
        gring = sb("gring", NGATHER * D)
        keep = sb("keep", 6144)
        work = sb("work", 7232)
        diags = sb("diags", 4 * 128)
        sel_idx = sb("sel_idx", 2 * 128, U32)
        sel_g = sb("sel_g", 2 * 128)
        acts = sb("acts", 2 * 128)
        ipos = sb("ipos", 4, I32)

        V, A, T, G, S = (Queue(sem(n)) for n in ("s_v", "s_a", "s_t", "s_g", "s_s"))
        banks = Ring([Slot(PS[:, 512 * i:512 * (i + 1)]) for i in range(6)])
        ybank = [PS[:, 512 * i:512 * (i + 1)] for i in (6, 7)]
        wslots = Ring([Slot(wring[:, 2048 * i:2048 * (i + 1)], sem(f"s_w{i}")) for i in range(NWS)])
        gslots = Ring([Slot(gring[:, D * i:D * (i + 1)], sem(f"s_u{i}")) for i in range(NGATHER)])
        dslots = Ring([Slot(diags[:, 128 * i:128 * (i + 1)]) for i in range(4)])
        outs = Slot(None, sem("s_out"))

        ident = consts[:, C_ID:C_ID + 128]
        mask = consts[:, C_MASK:C_MASK + 2048].rearrange("p (g t s) -> p g t s", g=4, t=2)
        iota = consts[:, C_IOTA:C_IOTA + 16]
        x = [xs[:, D * t:D * (t + 1)] for t in range(2)]
        h = [hs[:, D * t:D * (t + 1)] for t in range(2)]
        hT = hTs[:, :].rearrange("p (k s) -> p k s", k=8)
        gain = [gains[:, D * i:D * (i + 1)] for i in range(6)]
        cc = tabs[:, 0:224].rearrange("p (t c) -> p t c", t=2)
        ss = tabs[:, 224:448].rearrange("p (t c) -> p t c", t=2)
        xtok = [None, None]

        def bar():
            ends = [(id(q), q.sem, q.n) for q in (V, A, T, G) if q.n]
            for q in (V, A, T, G):
                q.wait(*ends)
            return ends

        def bcast(ap, n):
            return ap.partition_broadcast(128)

        def load(slot, dst, src, *tok):
            return S.dma(lambda e: e.dma_start(dst, src), slot, *tok)

        def load_group(name, *pairs):
            g = Slot(None, sem(name))
            for dst, src in pairs:
                t = load(g, dst, src)
            return t

        cw = keep[:, 0:128]
        cT8 = small[:, 0:8]
        crow = keep[0:8, 128:256]
        mod = gring[:, 0:6 * D]
        poolB = gring[:, 6 * D:8 * D].rearrange("p (s g t) -> p s g t", s=2, g=4)
        bp = gring[:, 8 * D:8 * D + 512]
        wp = gring[0:64, 8 * D + 512:8 * D + 768].rearrange("p (g c) -> p g c", g=4)
        tc_ = load_group("s_l0", (crow, a["c"].rearrange("o (r c) -> (o r) c", c=128)), (ident, a["consts"][:, 0:128]),
                         (cw[0:66, :], a["conv_w"][0].rearrange("t (j c) -> (t j) c", c=128)),
                         (cw[66:88, :], a["conv_b"].rearrange("o (j c) -> (o j) c", c=128)))
        for q in (V, A, T, G):
            q.wait(tc_)

        def loads_gains():
            t = load_group("s_l3", (mod[:, 4096:6144], a["b_ada"][0, 4096:6144].partition_broadcast(128)),
                           *((gain[i], a[n][0].partition_broadcast(128)) for i, n in
                             ((1, "g_post_mix"), (2, "g_pre_ffn"), (3, "g_post_ffn"))))
            return t

        def loads_pool():
            return load_group("s_l5", (gring[:, 6 * D:8 * D], a["pool_band"]),
                              (bp[:, 0:256], a["b_pool"][0].rearrange("g c -> (g c)").partition_broadcast(128)),
                              (bp[:, 256:512], a["pool_scale"][0].partition_broadcast(128)),
                              (wp, a["w_pool"][0].rearrange("g c d -> c g d")))

        def load_w(parts):
            s = wslots.take()
            view = s.ap.rearrange("p (k n) -> p k n", n=512)
            tok = None
            for col, w, r0, nk, c0, n in parts:
                src = w[r0:r0 + 128 * nk, c0:c0 + n].rearrange("(k p) n -> p k n", p=128)
                tok = S.dma(lambda e, d=view[:, 0:nk, col:col + n], src=src: e.dma_start(d, src), s, s.free)
            return s, view, tok

        def project(tiles, lhs, ltok, w, K, cols, evac):
            kt = K // 128
            for c0, n in cols:
                bk = {t: banks.take() for t in tiles}
                for k0 in range(0, kt, 4):
                    nk = min(4, kt - k0)
                    s, view, tok = load_w([(0, w, 128 * k0, nk, c0, n)])
                    for t in tiles:
                        for k in range(nk):
                            m = T(lambda e, o=bk[t].ap[:, 0:n], l=lhs(k0 + k, t), r=view[:, k, 0:n],
                                  a0=(k0 + k == 0), z=(k0 + k == kt - 1): e.matmul(o, l, r, start=a0, stop=z),
                                  tok, ltok[t] if isinstance(ltok, dict) else ltok, bk[t].free, inc=(k == nk - 1))
                        if k0 + nk == kt:
                            bk[t].done = m
                        yield 0.85 * nk
                    s.free = [m]
                for t in tiles:
                    bk[t].free = evac(t, c0, n, bk[t].ap[:, 0:n], bk[t].done)

        flip = [0, 2]

        def copy(dst, src, *tok):
            flip[0] += 1
            if flip[0] % flip[1]:
                return A(lambda e: e.activation(dst, src, ACT.Copy), *tok)
            return V(lambda e: e.tensor_copy(dst, src), *tok)

        def transposes(srcs, dst, tok, wtok=None):
            toks = []
            for i0 in range(0, len(srcs), 4):
                grp = srcs[i0:i0 + 4]
                b = banks.take()
                c = grp[0].shape[1]
                for i, s in enumerate(grp):
                    m = T(lambda e, o=b.ap[0:c, 128 * i:128 * i + 128], s=s: e.transpose(o, s, ident),
                          tok, b.free, inc=(i == len(grp) - 1))
                t = copy(dst(i0, len(grp)), b.ap[0:c, 0:128 * len(grp)].rearrange("p (b q) -> p b q", q=128), m, wtok)
                b.free = [t]
                toks.append(t)
            return toks

        nsm = [32]

        def sm(n):
            if nsm[0] + n > 512:
                nsm[0] = 32
            nsm[0] += n
            return small[:, nsm[0] - n:nsm[0]]

        def rstd(srcs, n, junks, *tok, whole=True):
            m = len(srcs)
            s = sm(8 * m)
            c = [s[:, m * i:m * (i + 1)] for i in range(8)]
            t = [A(lambda e, i=i, a_=a_, b_=b_: e.activation(b_, a_, ACT.Square, accum_out=c[0][:, i:i + 1]), *tok)
                 for i, (a_, b_) in enumerate(zip(srcs, junks))]
            t = V(lambda e: e.tensor_scalar(c[1], c[0], 1.0 / n, EPS, ALU.mult, ALU.add), t)
            t = A(lambda e: e.activation(c[2], c[1], ACT.Sqrt), t)
            return rstd_end(c, t) if whole else (c, t)

        def rstd_end(c, t):
            t = V(lambda e: e.reciprocal(c[3], c[2]), t)
            t = V(lambda e: e.tensor_tensor(c[4], c[3], c[3], ALU.mult), t)
            t = V(lambda e: e.tensor_tensor(c[5], c[4], c[1], ALU.mult), t)
            t = V(lambda e: e.tensor_scalar(c[6], c[5], -0.5, 1.5, ALU.mult, ALU.add), t)
            t = V(lambda e: e.tensor_tensor(c[7], c[3], c[6], ALU.mult), t)
            return c[7], t

        def norm(dst, src, g, n, junk, *tok):
            r, t = rstd([src], n, [junk], *tok)
            return V(lambda e: e.scalar_tensor_tensor(dst, src, r, g, ALU.mult, ALU.mult), t)

        att_bufs = [Ring([Slot(work[:, 768 * i:768 * (i + 1)]) for i in range(3)]),
                    Ring([Slot(work[:, o:o + 768]) for o in (2304, 6144)])]

        def att_scores(tile, segs, scale, tok):
            nk = 128 * (tile + 1)
            n = len(segs)
            buf = att_bufs[0].take()
            s = sm(8)
            tt = []
            for g, (q, k, v, m) in enumerate(segs):
                b = banks.take()
                t = T(lambda e, o=b.ap[:, 0:nk], q=q, k=k[:, 0:nk]: e.matmul(o, q, k, start=True, stop=True),
                      tok, b.free)
                t = V(lambda e, o=buf.ap[:, nk * g:nk * g + nk], i=b.ap[:, 0:nk], m=m[:, 0:nk], r=s[:, g:g + 1]:
                      e.tensor_tensor_reduce(o, i, m, 1.0, LOW, ALU.add, ALU.max, r), t, buf.free)
                b.free = [t]
            if n > 1:
                t = V(lambda e: e.tensor_reduce(s[:, 3:4], s[:, 0:n], AX.X, ALU.max), t)
                top = s[:, 3:4]
            else:
                top = s[:, 0:1]
            t = V(lambda e: e.tensor_scalar(s[:, 4:5], top, -scale, None, ALU.mult), t)
            p = buf.ap[:, 0:nk * n]
            t = A(lambda e: e.activation(p, p, ACT.Exp, bias=s[:, 4:5], scale=scale, accum_out=s[:, 5:6]), t)
            return tile, segs, buf, s, t

        def att_turn(state):
            tile, segs, buf, s, te = state
            tr = V(lambda e: e.reciprocal(s[:, 6:7], s[:, 5:6]), te)
            pt = att_bufs[1].take()
            nb = (tile + 1) * len(segs)
            ptv = pt.ap.rearrange("p (b q) -> p b q", q=128)
            tk = transposes([buf.ap[:, 128 * i:128 * i + 128] for i in range(nb)],
                            lambda i0, n: ptv[:, i0:i0 + n, :], te, pt.free)
            buf.free = [(id(T), T.sem, T.n)]
            return tile, segs, pt, ptv, s, tk, tr

        def att_values(state, dst):
            tile, segs, pt, ptv, s, tk, tr = state
            nt = tile + 1
            nb = nt * len(segs)
            b = banks.take()
            for i in range(nb):
                v = segs[i // nt][2](i % nt)
                t = T(lambda e, o=b.ap[:, 0:64], l=ptv[:, i, :], v=v, i=i: e.matmul(o, l, v, start=(i == 0),
                      stop=(i == nb - 1)), tk, b.free, inc=(i == nb - 1))
            pt.free = [t]
            t = V(lambda e, o=b.ap[:, 0:64]: e.tensor_scalar(dst, o, s[:, 6:7], None, ALU.mult), t, tr)
            b.free = [t]

        tiles_n = [0]

        def attention(units, tok):
            scored, turned = [], []
            for u in chain(units, [None, None]):
                if u:
                    tiles_n[0] = u[0]
                    scored.append((att_scores(u[0], u[1], u[2], tok), u[3]))
                if len(scored) > (1 if u else 0):
                    st, dst = scored.pop(0)
                    turned.append((att_turn(st), dst))
                if len(turned) > (1 if u else 0):
                    att_values(*turned.pop(0))
                yield 3.0 + 1.5 * tiles_n[0]

        TR16, TR64, TR32 = (0, 16), (16, 64), (80, 32)

        def rope(dst, src, tile, which, heads, b1, b2, *tok):
            o, w = which
            hw = w // 2
            c = cc[:, tile, o:o + w].unsqueeze(1).to_broadcast([128, heads, w])
            s0 = ss[:, tile, o:o + hw].unsqueeze(1).to_broadcast([128, heads, hw])
            s1 = ss[:, tile, o + hw:o + w].unsqueeze(1).to_broadcast([128, heads, hw])
            va = b1[:, 0:heads * w].rearrange("p (h w) -> p h w", w=w)
            vb = b2[:, 0:heads * w].rearrange("p (h w) -> p h w", w=w)
            V(lambda e: e.tensor_tensor(va, src, c, ALU.mult), *tok)
            V(lambda e: e.tensor_tensor(vb[:, :, 0:hw], src[:, :, hw:w], s0, ALU.mult))
            t = V(lambda e: e.tensor_tensor(vb[:, :, hw:w], src[:, :, 0:hw], s1, ALU.mult))
            return t, V(lambda e: e.tensor_tensor(dst, va, vb, ALU.add), t)

        def run(gen):
            for _ in gen:
                pass

        s = sm(32)
        b = banks.take()
        T(lambda e: e.transpose(b.ap[:, 0:8], crow, ident[0:8, 0:8]), inc=False)
        t = T(lambda e: e.transpose(b.ap[:, 128:216], cw[0:88, :], ident[0:88, 0:88]))
        cwT = keep[:, 256:344]
        V(lambda e: e.tensor_copy(cT8, b.ap[:, 0:8]), t)
        t = V(lambda e: e.tensor_copy(cwT, b.ap[:, 128:216]), t)
        b.free = [t]
        t = A(lambda e: e.activation(s[:, 0:8], cT8, ACT.Exp, scale=-1.0), t)
        t = V(lambda e: e.tensor_scalar(s[:, 8:16], s[:, 0:8], 1.0, None, ALU.add), t)
        t = V(lambda e: e.reciprocal(s[:, 16:24], s[:, 8:16]), t)
        cact = small[:, 12:20]
        tcact = V(lambda e: e.tensor_tensor(cact, s[:, 16:24], cT8, ALU.mult), t)
        ones = keep[:, 384:512]
        to = V(lambda e: e.memset(ones, 1.0))
        A.wait(V(lambda e: e.memset(small[:, 20:22], 1.0)))
        accs = Ring([Slot(gain[4][:, 512 * i:512 * i + 512]) for i in range(2)])
        early = []

        def warm(f, *tok):
            A(lambda e: e.activation(small[:, 22:23], small[:, 20:21], f), *tok)

        def modulation():
            def total(i, ac, tv):
                b = banks.take()
                tm = T(lambda e: e.matmul(b.ap, ones, ac.ap, start=True, stop=True), tv, to, b.free)
                ac.free = [tm]
                return i, b, tm

            def finish(i, b, tm, bias):
                mc = mod[:, 512 * i:512 * i + 512]
                tv = V(lambda e: e.tensor_tensor(mc, b.ap, mc, ALU.add), tm, bias)
                b.free = [tv]

            summed, bias, kept = None, None, []
            for i in range(12):
                ac = accs.take()
                for g in range(2):
                    sl, view, tok = load_w([(0, a["w_ada"][0], 512 * g, 4, 512 * i, 512)])
                    if (i, g) == (2, 1):
                        bias = load_group("s_l2", (mod[:, 0:2048], a["b_ada"][0, 0:2048].partition_broadcast(128)),
                                          (gain[0], a["g_pre_mix"][0].partition_broadcast(128)))
                    if (i, g) == (1, 1):
                        early.append(load_group("s_l1", (x[0], a["x"][0, 0:128, :]), (x[1], a["x"][0, 128:256, :])))
                    if (i, g) == (4, 1):
                        bias = load_group("s_l7", (mod[:, 2048:4096], a["b_ada"][0, 2048:4096]
                                                   .partition_broadcast(128)))
                    if (i, g) == (8, 1):
                        bias = loads_gains()
                    for k in range(4 * g, 4 * g + 4):
                        if k == 0:
                            tv = V(lambda e, ac=ac, view=view: e.tensor_scalar(
                                ac.ap, view[:, 0, :], cact[:, 0:1], None, ALU.mult), tok, ac.free, tcact)
                        else:
                            tv = V(lambda e, k=k, ac=ac, view=view: e.scalar_tensor_tensor(
                                ac.ap, view[:, k % 4, :], cact[:, k:k + 1], ac.ap, ALU.mult, ALU.add), tok, tv)
                    sl.free = [tv]
                    if g == 0:
                        yield
                if summed:
                    kept.append(total(*summed))
                summed = (i, ac, tv)
                if i in (9, 11):
                    yield
                if i in (3, 7, 9, 11):
                    kept.append(total(*summed))
                    summed = None
                while kept and i > 2:
                    finish(*kept.pop(0), bias)
                yield

        sh_m, sc_m, gt_m, sh_f, sc_f, gt_f = (mod[:, D * i:D * (i + 1)] for i in range(6))
        mods = modulation()
        for _ in range(6):
            next(mods)
        rx, t = rstd(x, D, h, early, whole=False)
        for _ in range(2):
            next(mods)
        rx, _ = rstd_end(rx, t)
        tables = load_group("s_l6", (consts[:, 128:C_END], a["consts"][:, 128:C_END]), (ipos[:, :], a["pos"]))
        trx = V(lambda e: e.scalar_tensor_tensor(sc_m, sc_m, 1.0, gain[0], ALU.add, ALU.mult),
                (id(V), V.sem, V.n))

        def modulated(r, tr, sc, sh, tiles=(0, 1)):
            done = []
            for n, tl in enumerate(tiles):
                t = V(lambda e, tl=tl, n=n: e.scalar_tensor_tensor(h[tl], x[tl], r[:, n:n + 1], sc, ALU.mult,
                                                                   ALU.mult), tr)
                t = V(lambda e, tl=tl: e.tensor_tensor(h[tl], h[tl], sh, ALU.add), t)
                done += transposes([h[tl][:, 128 * i:128 * i + 128] for i in range(8)],
                                   lambda i0, n, tl=tl: hT[:, i0:i0 + n, 128 * tl:128 * tl + 128], t)
            return done

        th = {0: modulated(rx, trx, sc_m, sh_m, (0,))}
        proj = keep[:, 1024:6144].rearrange("p (t c) -> p t c", t=2)

        tproj = [[], []]

        def ev_proj(t, c0, n, ps, tok):
            tproj[t].append(copy(proj[:, t, c0:c0 + n], ps, tok))
            if c0 == 1536:
                src = proj[:, t, 256:1792].rearrange("p (h w) -> p h w", w=64)[:, :, 0:16]
                o = 1024 * t
                _, trope[t] = rope(src, src, t, TR16, 24, work[:, o:o + 384], work[:, o + 512:o + 896], tproj[t])
            return [tproj[t][-1]]

        trope = [None, None]
        ins = project([0, 1], lambda k, t: hT[:, k, 128 * t:128 * t + 128], th, a["w_in"][0], D,
                      [(512 * i, 512) for i in range(5)], ev_proj)
        next(ins)
        th[1] = modulated(rx[:, 1:2], trx, sc_m, sh_m, (1,))
        V.wait(tables)
        angb = work[:, 0:1120].rearrange("p (b t c) -> p b t c", b=5, t=2)
        t = V(lambda e: e.tensor_copy(small[:, 8:12], ipos[:, 0:4]))
        freq = consts[:, C_FREQ:C_FREQ + 112]
        sgn = consts[:, C_SGN:C_SGN + 112]
        for tl in range(2):
            V(lambda e, tl=tl: e.tensor_scalar(angb[:, 0, tl, 0:16], freq[:, 0:16], small[:, 8 + tl:9 + tl], None,
                                               ALU.mult), t)
            V(lambda e, tl=tl: e.tensor_scalar(angb[:, 0, tl, 16:112], freq[:, 16:112],
                                               small[:, 10 + tl:11 + tl], None, ALU.mult), t)
        P2 = 2.0 * np.pi
        C1 = 6.28125
        C2 = float(np.float32(np.round((P2 - C1) * 2 ** 22) / 2 ** 22))
        C3 = float(np.float32(P2 - C1 - C2))
        MG = 12582912.0
        PI = float(np.nextafter(np.float32(np.pi), np.float32(0)))
        for dstt, shift, back in ((ss, 0.0, 0.0), (cc, 0.25, float(np.float32(np.pi / 2)))):
            ang, n1, r1, r2 = (angb[:, i, :, :] for i in range(4))
            t = (id(V), V.sem, V.n)
            t = V(lambda e, shift=shift: e.tensor_scalar(n1, ang, 1.0 / P2, shift, ALU.mult, ALU.add), t)
            t = V(lambda e: e.tensor_scalar(n1, n1, MG, None, ALU.add), t)
            t = V(lambda e: e.tensor_scalar(n1, n1, -MG, None, ALU.add), t)
            t = V(lambda e: e.scalar_tensor_tensor(r1, n1, -C1, ang, ALU.mult, ALU.add), t)
            t = V(lambda e: e.scalar_tensor_tensor(r2, n1, -C2, r1, ALU.mult, ALU.add), t)
            t = V(lambda e: e.scalar_tensor_tensor(r1, n1, -C3, r2, ALU.mult, ALU.add), t)
            t = V(lambda e, back=back: e.tensor_scalar(r2, r1, back, PI, ALU.add, ALU.min), t)
            t = V(lambda e: e.tensor_scalar(r1, r2, -PI, None, ALU.max), t)
            ta = A(lambda e, dstt=dstt: e.activation(dstt, r1, ACT.Sin), t)
            V.wait(ta)
        V(lambda e: e.tensor_tensor(ss, ss, sgn.unsqueeze(1).to_broadcast([128, 2, 112]), ALU.mult), ta)
        for n, _ in enumerate(ins, 1):
            if n % 2 == 1 and n < 16:
                next(mods)
            if n == 14:
                tpool = loads_pool()
        cat = hs[:, 0:1024].rearrange("p (t c) -> p t c", t=2)
        mixT = hs[0:64, 1024:2048].rearrange("p (g t) -> p g t", g=4)
        T.wait(tpool, [t[0] for t in tproj])
        V.wait(tpool)
        tmix = []
        for g in range(4):
            b = banks.take()
            for si in range(2):
                t = T(lambda e, g=g, si=si, b=b: e.matmul(b.ap[0:64, 0:256], proj[:, si, 64 * g:64 * g + 64],
                      poolB[:, si, g, :], start=(si == 0), stop=(si == 1)), b.free, inc=(si == 1))
            t = copy(mixT[:, g, :], b.ap[0:64, 0:256], t)
            b.free = [t]
            tmix.append(t)
        qkT = work[:, 3072:6144].rearrange("p (b s) -> p b s", b=12)
        for tl in range(2):
            transposes([proj[:, tl, 256 + 128 * i:384 + 128 * i] for i in range(12)],
                       lambda i0, n, tl=tl: qkT[:, i0:i0 + n, 128 * tl:128 * tl + 128], trope[tl])
        T.wait(tmix)
        for tl in range(2):
            b = banks.take()
            for g in range(4):
                t = T(lambda e, g=g, tl=tl, b=b: e.matmul(b.ap[:, 64 * g:64 * g + 64],
                      mixT[:, g, 128 * tl:128 * tl + 128], wp[:, g, :], start=True, stop=True), b.free, inc=(g == 3))
            t = V(lambda e, tl=tl, b=b: e.tensor_tensor(cat[:, tl, 0:256], b.ap[:, 0:256], bp[:, 0:256], ALU.add), t)
            b.free = [t]
            V(lambda e, tl=tl: e.tensor_tensor(cat[:, tl, 0:256], cat[:, tl, 0:256], bp[:, 256:512], ALU.mult), t)
        bar()
        units = []
        for tl in range(2):
            for hh in range(4):
                segs = []
                for g in range(3):
                    hd = 4 * g + hh
                    r = 64 * (hd % 2)
                    segs.append((qkT[r:r + 64, hd // 2, 128 * tl:128 * tl + 128], qkT[r:r + 64, 6 + hd // 2, :],
                                 (lambda kt, hd=hd: proj[:, kt, 1792 + 64 * hd:1856 + 64 * hd]), mask[:, g, tl, :]))
                units.append((tl, segs, 0.125, cat[:, tl, 256 + 64 * hh:320 + 64 * hh]))
        for n, _ in enumerate(attention(units, None)):
            if n % 2 and n < 10:
                next(mods)
        warm(ACT.Sqrt)
        V(lambda e: e.scalar_tensor_tensor(sc_f, sc_f, 1.0, gain[2], ALU.add, ALU.mult), (id(V), V.sem, V.n))
        V(lambda e: e.tensor_tensor(gt_m, gt_m, gain[1], ALU.mult))
        bar()
        tcat = [transposes([cat[:, tl, 128 * i:128 * i + 128] for i in range(4)],
                           lambda i0, n, tl=tl: hT[:, i0:i0 + n, 128 * tl:128 * tl + 128], None) for tl in range(2)]
        ybuf = work[:, 3072:5120].rearrange("p (t c) -> p t c", t=2)
        tys = [[], []]

        def ev_y(t, c0, n, ps, tok):
            tys[t].append(copy(ybuf[:, t, c0:c0 + n], ps, tok))
            return [tys[t][-1]]

        def apart(lhs, w, K, cols):
            kt = K // 128
            groups = [(c0, n, [load_w([(0, w, 128 * k0, min(4, kt - k0), c0, n)]) for k0 in range(0, kt, 4)])
                      for c0, n in cols]
            done = [[], []]
            for t in range(2):
                for c0, n, slots in groups:
                    b = banks.take()
                    for k in range(kt):
                        sl, view, tok = slots[k // 4]
                        m = T(lambda e, b=b, k=k, t=t, n=n, view=view: e.matmul(
                            b.ap[:, 0:n], lhs(k, t), view[:, k % 4, 0:n], start=(k == 0), stop=(k == kt - 1)),
                            tok, b.free, tcat[t], inc=(k % 4 == 3 or k == kt - 1))
                        sl.free = [m]
                    done[t].append((c0, n, b, m))

            def out_(t):
                for c0, n, b, m in done[t]:
                    b.free = ev_y(t, c0, n, b.ap[:, 0:n], m)
            return out_

        take_out = apart(lambda k, t: hT[:, k, 128 * t:128 * t + 128], a["w_out"][0], 512, [(0, 512), (512, 512)])

        def y_scale(tl):
            return rstd([ybuf[:, tl, :]], D, [h[tl]], tys[tl])

        def add_y(tl, gt, r, t):
            y = ybuf[:, tl, :]
            t = V(lambda e: e.scalar_tensor_tensor(y, y, r, gt, ALU.mult, ALU.mult), t)
            return V(lambda e: e.tensor_tensor(x[tl], x[tl], y, ALU.add), t)

        def out_chain(tl):
            take_out(tl)
            yield
            r, t = y_scale(tl)
            yield
            t = add_y(tl, gt_m, r, t)
            yield
            r, t = rstd([x[tl]], D, [h[tl]], t)
            yield
            yield modulated(r, t, sc_f, sh_f, (tl,))

        first_, second_ = out_chain(0), out_chain(1)
        for g in (first_, first_, first_, second_, first_, second_, second_):
            next(g)
        gT = keep[:, 512:512 + 22 * 256].rearrange("p (j s) -> p j s", j=22)
        cbuf = Ring([Slot(work[:, 1024 + 512 * i:1024 + 512 * (i + 1)]) for i in range(4)])

        def up_products(bg, bv, halves, c0, n, tok_h):
            for b, off in ((bg, 0), (bv, 256)):
                for j in range(2):
                    for k in range(8):
                        sl, view, tok = halves[k // 4]
                        m = T(lambda e, b=b, j=j, k=k, off=off, view=view: e.matmul(
                            b.ap[:, 256 * j + c0:256 * j + c0 + n], view[:, k % 4, off + 128 * j:off + 128 * j + 128],
                            hT[:, k, c0:c0 + n], start=(k == 0), stop=(k == 7)), tok, b.free, tok_h,
                            inc=(k == 7 and j == 1))
                b.done = m
            return m

        for ch in range(11):
            halves = [load_w([(0, a["w_up"][0], 512 * g, 4, 256 * ch, 256),
                              (256, a["w_up"][0], 512 * g, 4, D_FF + 256 * ch, 256)]) for g in range(2)]
            bg, bv = banks.take(), banks.take()
            if ch:
                m = up_products(bg, bv, halves, 0, 256, None)
            else:
                up_products(bg, bv, halves, 0, 128, next(first_))
                next(second_)
                m = up_products(bg, bv, halves, 128, 128, next(second_))
            for sl, _, _ in halves:
                sl.free = [m]
            cs = cbuf.take()
            for j in range(2):
                jj = 2 * ch + j
                acc = cs.ap[:, 256 * j:256 * j + 256]
                gp = bg.ap[:, 256 * j:256 * j + 256]
                t = V(lambda e, acc=acc, gp=gp, jj=jj: e.tensor_scalar(acc, gp, cwT[:, 44 + jj:45 + jj],
                      cwT[:, 66 + jj:67 + jj], ALU.mult, ALU.add), bg.done, cs.free)
                t = V(lambda e, acc=acc, gp=gp, jj=jj: e.scalar_tensor_tensor(acc[:, 1:256], gp[:, 0:255],
                      cwT[:, 22 + jj:23 + jj], acc[:, 1:256], ALU.mult, ALU.add), t)
                t = V(lambda e, acc=acc, gp=gp, jj=jj: e.scalar_tensor_tensor(acc[:, 2:256], gp[:, 0:254],
                      cwT[:, jj:jj + 1], acc[:, 2:256], ALU.mult, ALU.add), t)
            bg.free = [t]
            t = A(lambda e, cs=cs: e.activation(cs.ap, cs.ap, ACT.Gelu_apprx_tanh), t)
            t = V(lambda e, cs=cs, bv=bv, ch=ch: e.tensor_tensor(gT[:, 2 * ch:2 * ch + 2, :],
                  cs.ap.rearrange("p (j s) -> p j s", j=2), bv.ap.rearrange("p (j s) -> p j s", j=2), ALU.mult),
                  t, bv.done)
            bv.free = [t]
            cs.free = [t]
            if 1 <= ch <= 5:
                next(mods)
            if ch == 5:
                tgain = V(lambda e: e.tensor_tensor(gt_f, gt_f, gain[3], ALU.mult), (id(V), V.sem, V.n))
        T.wait(t)
        warm(ACT.Sqrt)
        loads2 = Slot(None, sem("s_l4"))
        for i, (n, r) in enumerate((("attn_norm_2", 0), ("ffn_norm_2", 0), ("attn_norm_2", 1), ("ffn_norm_2", 1))):
            load(loads2, gain[i], a[n][r].partition_broadcast(128), tgain)
        load(loads2, gain[4], a["final_norm_2"].partition_broadcast(128))
        load(loads2, gain[5][:, 0:768], a["mla_q_norm_2"][0].partition_broadcast(128))
        ldg = load(loads2, gain[5][:, 768:1024], a["mla_kv_norm_2"][0].partition_broadcast(128))
        V.wait((id(V), V.sem, V.n))
        lhsG = lambda k, t: gT[:, k, 128 * t:128 * t + 128]
        tys[0].clear()
        tys[1].clear()
        run(project([0, 1], lhsG, None, a["w_down"][0], D_FF, [(0, 512)], ev_y))
        take_out = apart(lhsG, a["w_down"][0], D_FF, [(512, 512)])
        take_out(0)
        xtok[0] = add_y(0, gt_f, *y_scale(0))
        V.wait(ldg)
        tnorm = norm(h[0], x[0], gain[0], D, h[0], xtok[0])
        take_out(1)

        flip[1] = 4
        att_bufs[0] = Ring([Slot(work[:, 256 * i:256 * (i + 1)]) for i in range(4)])
        att_bufs[1] = Ring([Slot(work[:, 1024 + 256 * i:1280 + 256 * i]) for i in range(4)])
        lhsD = lambda k, t: hT[:, k, 0:128]

        def dense_bar():
            ends = [(id(q), q.sem, q.mark) for q in (V, A, T)]
            for q in (V, A, T):
                q.wait(*ends)

        def to_hT(src, nb, tok, at=0):
            return transposes([src[:, 128 * i:128 * i + 128] for i in range(nb)],
                              lambda i0, n: hT[:, at + i0:at + i0 + n, 0:128], tok)

        def add_x(tile):
            def ev(t, c0, n, ps, tok):
                xt = x[tile][:, c0:c0 + n]
                return [V(lambda e: e.tensor_tensor(xt, ps, xt, ALU.add), tok)]
            return ev

        kT6 = keep[:, 0:1536].rearrange("p (b s) -> p b s", b=6)
        vals = keep[:, 1536:2688].rearrange("p (t c) -> p t c", t=2)
        HY = [(0, 512), (512, 128), (640, 512), (1152, 72), (1224, 512), (1736, 512), (2248, 512)]

        def hybrid(tile, t=None):
            t = t or norm(h[tile], x[tile], gain[0], D, h[tile], xtok[tile])
            yield 3.0
            to_hT(h[tile], 8, t)
            yield 3.0
            dense_bar()
            pj = work[:, 3072:5632]
            rb = Ring([Slot(work[:, 512 * i:512 * i + 1024 - 512]) for i in range(6)])
            iw = sm(8)

            def ev(t, c0, n, ps, tok):
                spots = {0: (0, 512), 512: (1536, 64), 640: (512, 512), 1152: (1664, 64), 1224: (1024, 512),
                         1736: (1792, 512)}
                rd = []
                if c0 == 2248:
                    return [copy(vals[:, tile, 64:576], ps, tok)]
                at, w = spots[c0]
                r1, r2 = rb.take(), rb.take()
                hd = w // 64
                t3, t4 = rope(pj[:, at:at + w].rearrange("p (h w) -> p h w", w=64),
                              ps[:, 0:w].rearrange("p (h w) -> p h w", w=64), tile, TR64, hd, r1.ap, r2.ap, tok)
                rd.append(t3)
                if c0 in (512, 1152):
                    V(lambda e: e.tensor_copy(pj[:, at + 64:at + 128], pj[:, at:at + 64]), t4)
                if c0 == 512:
                    rd.append(copy(vals[:, tile, 0:64], ps[:, 64:128], t3))
                if c0 == 1152:
                    rd.append(copy(iw, ps[:, 64:72], t3))
                return rd

            yield from project([tile], lhsD, None, a["hyb_w_in_2"][0], D, HY, ev)
            dense_bar()
            qT = hTs[:, 0:1536].rearrange("p (b s) -> p b s", b=12)
            sl = slice(128 * tile, 128 * tile + 128)
            transposes([pj[:, 128 * i:128 * i + 128] for i in range(12)], lambda i0, n: qT[:, i0:i0 + n, :], None)
            transposes([pj[:, 1536 + 128 * i:1664 + 128 * i] for i in range(6)],
                       lambda i0, n: kT6[:, i0:i0 + n, sl], None)
            dense_bar()
            yield
            nk = 128 * (tile + 1)
            score = work[:, 3072:3072 + nk]
            sel = work[:, 3328:3328 + nk]
            rl = Ring([Slot(work[:, 3584 + 256 * i:3584 + 256 * i + nk]) for i in range(2)])
            for g in range(8):
                r = 64 * (g % 2)
                b = banks.take()
                t = T(lambda e, b=b, g=g, r=r: e.matmul(b.ap[:, 0:nk], qT[r:r + 64, 4 + g // 2, :],
                      kT6[r:r + 64, 1, 0:nk], start=True, stop=True), b.free)
                q = rl.take()
                t = A(lambda e, b=b, q=q: e.activation(q.ap, b.ap[:, 0:nk], ACT.Relu), t, q.free)
                b.free = [t]
                if g == 0:
                    t = V(lambda e, q=q: e.tensor_scalar(score, q.ap, iw[:, 0:1], None, ALU.mult), t)
                else:
                    t = V(lambda e, q=q, g=g: e.scalar_tensor_tensor(score, q.ap, iw[:, g:g + 1], score, ALU.mult,
                                                                     ALU.add), t, tv)
                tv = t
                q.free = [t]
            wsc = float(np.float32(8 ** -0.5 * 64 ** -0.5))
            t = V(lambda e: e.scalar_tensor_tensor(score, score, wsc, mask[:, 3, tile, 0:nk], ALU.mult, ALU.add), t)
            yield
            ob = work[:, 4608:5632]

            def units(t):
                for g in range(8):
                    m8 = sm(8)
                    t = V(lambda e, m8=m8: e.max(m8, score), t)
                    t = V(lambda e, m8=m8: e.match_replace(score, m8, score, LOW), t)
                    r = 64 * (g % 2)
                    yield (tile, [(qT[r:r + 64, 8 + g // 2, :], kT6[r:r + 64, 2 + g // 2, :],
                                   (lambda kt, g=g: vals[:, kt, 64 + 64 * g:128 + 64 * g]), mask[:, 3, tile, :])],
                           0.125, ob[:, 512 + 64 * g:576 + 64 * g])
                t = V(lambda e: e.tensor_scalar(sel, score, LOW, 1.0, ALU.is_equal, ALU.subtract), t)
                t = V(lambda e: e.tensor_scalar(sel, sel, 1.0e30, None, ALU.mult), t)
                V.wait(V(lambda e: e.tensor_tensor(sel, sel, mask[:, 3, tile, 0:nk], ALU.add), t))
                for g in range(8):
                    r = 64 * (g % 2)
                    yield (tile, [(qT[r:r + 64, g // 2, :], kT6[r:r + 64, 0, :],
                                   (lambda kt: vals[:, kt, 0:64]), sel)], 0.125, ob[:, 64 * g:64 * g + 64])

            yield from attention(units(t), None)
            dense_bar()
            to_hT(ob, 8, None)
            dense_bar()
            yield from project([tile], lhsD, None, a["hyb_w_out_2"][0], D, [(0, 512), (512, 512)], add_x(tile))
            dense_bar()

        mkT = keep[:, 0:4096].rearrange("p (b s) -> p b s", b=16)
        mv = keep[:, 4096:6144].rearrange("p (t c) -> p t c", t=2)

        def mla(tile):
            sl = slice(128 * tile, 128 * tile + 128)
            t = norm(h[tile], x[tile], gain[2], D, h[tile], xtok[tile])
            yield 3.0
            to_hT(h[tile], 8, t)
            yield 3.0
            dense_bar()
            lin = work[:, 6144:7200]

            def ev(t, c0, n, ps, tok):
                return [copy(lin[:, c0:c0 + n], ps, tok)]

            yield from project([tile], lhsD, None, a["mla_w_in_2"][0], D, [(0, 512), (512, 512), (1024, 32)], ev)
            dense_bar()
            t1 = norm(lin[:, 0:768], lin[:, 0:768], gain[5][:, 0:768], 768, h[tile][:, 0:768])
            t2 = norm(lin[:, 768:1024], lin[:, 768:1024], gain[5][:, 768:1024], 256, h[tile][:, 768:1024])
            krt = work[:, 7200:7232]
            kr = lin[:, 1024:1056].unsqueeze(1)
            rope(krt.unsqueeze(1), kr, tile, TR32, 1, h[tile][:, 0:32], h[tile][:, 32:64], t2)
            to_hT(lin, 8, t2)
            dense_bar()
            qf = work[:, 3072:4608]
            kf = work[:, 4608:6144].rearrange("p (h w) -> p h w", w=96)

            def ev_q(t, c0, n, ps, tok):
                return [copy(qf[:, c0:c0 + n], ps, tok)]

            def ev_kv(t, c0, n, ps, tok):
                i = c0 // 128
                v = ps.rearrange("p (h w) -> p h w", w=128)
                t1 = copy(kf[:, i:i + 4, 0:64], v[:, :, 0:64], tok)
                return [copy(mv[:, tile, 64 * i:64 * i + 256].rearrange("p (h w) -> p h w", w=64), v[:, :, 64:128],
                             t1)]

            yield from project([tile], lhsD, None, a["mla_w_uq_2"][0], 768, [(512 * i, 512) for i in range(3)], ev_q)
            yield from project([tile], lambda k, t: hT[:, 6 + k, 0:128], None, a["mla_w_ukv_2"][0], 256,
                               [(512 * i, 512) for i in range(4)], ev_kv)
            dense_bar()
            qv = qf.rearrange("p (h w) -> p h w", w=96)[:, :, 64:96]
            rope(qv, qv, tile, TR32, 16, h[tile][:, 0:512], h[tile][:, 512:1024])
            V(lambda e: e.tensor_copy(kf[:, :, 64:96], krt.unsqueeze(1).to_broadcast([128, 16, 32])))
            dense_bar()
            qT = hTs[0:96, :].rearrange("p (b s) -> p b s", b=16)
            transposes([qf[:, 96 * i:96 * i + 96] for i in range(16)], lambda i0, n: qT[:, i0:i0 + n, :], None)
            transposes([kf[:, i, :] for i in range(16)], lambda i0, n: mkT[0:96, i0:i0 + n, sl], None)
            dense_bar()
            yield
            ob = work[:, 3072:4096]
            units = [(tile, [(qT[:, g, :], mkT[0:96, g, :], (lambda kt, g=g: mv[:, kt, 64 * g:64 * g + 64]),
                      mask[:, 3, tile, :])], float(np.float32(96 ** -0.5)), ob[:, 64 * g:64 * g + 64])
                     for g in range(16)]
            yield from attention(units, None)
            dense_bar()
            to_hT(ob, 8, None)
            dense_bar()
            yield from project([tile], lhsD, None, a["mla_w_out_2"][0], D, [(0, 512), (512, 512)], add_x(tile))
            dense_bar()

        utab = a["peer_u_2"].rearrange("l n d -> (l n) d")
        vtab = a["peer_v_2"].rearrange("l n d -> (l n) d")

        def choose(tile, l):
            t = norm(h[tile], x[tile], gain[1 + 2 * l], D, h[tile])
            yield 3.0
            to_hT(h[tile], 8, t)
            yield 3.0
            dense_bar()
            kyT = work[:, 0:2048].rearrange("p (b n) -> p b n", b=16)
            qT = work[:, 2048:4096].rearrange("p (b n) -> p b n", b=16)
            qc = Slot(work[:, 6656:7168])
            flip[1] = 1 << 30
            s = wslots.take()
            kv = s.ap.rearrange("p (b c) -> p b c", b=16)
            src = a["peer_sub_keys_2"][l].rearrange("h t n c -> n (h t) c")
            tk = S.dma(lambda e: e.dma_start(kv, src), s, s.free)
            transposes([kv[:, i, :] for i in range(16)], lambda i0, n: kyT[:, i0:i0 + n, :], tk)
            s.free = [(id(T), T.sem, T.n)]

            turned = {}

            def ev(t, c0, n, ps, tok):
                tc = copy(qc.ap, ps, tok, qc.free)
                i = c0 // 128
                turned[i // 4] = transposes([qc.ap[:, 128 * j:128 * j + 128] for j in range(4)],
                                            lambda i0, n: qT[:, i + i0:i + i0 + n, :], tc)
                qc.free = [(id(T), T.sem, T.n)]
                return [tc]

            tv = work[:, 4096:4352].rearrange("p (b k) -> p b k", k=16)
            ti = work[:, 4352:4608].bitcast(U32).rearrange("p (b k) -> p b k", k=16)
            tmp = work[:, 6144:6656].rearrange("p (b n) -> p b n", b=4)
            def pick(g, b, t):
                sc = [b.ap[:, 128 * j:128 * j + 128] for j in range(4)]
                ks = [4 * g + j for j in range(4)]
                t1 = [V(lambda e, i=i, s=s: e.max(tv[:, i, 0:8], s), t) for i, s in zip(ks, sc)]
                for n, (i, s) in enumerate(zip(ks, sc)):
                    V(lambda e, i=i, s=s: e.max_index(ti[:, i, 0:8], tv[:, i, 0:8], s), t1[n])
                t2 = [V(lambda e, i=i, s=s: e.match_replace(tmp[:, i % 4, :], tv[:, i, 0:8], s, LOW))
                      for i, s in zip(ks, sc)]
                b.free = [t2[-1]]
                yield 3.0
                t3 = [V(lambda e, i=i: e.max(tv[:, i, 8:16], tmp[:, i % 4, :]), t2[n]) for n, i in enumerate(ks)]
                for n, i in enumerate(ks):
                    t = V(lambda e, i=i: e.max_index(ti[:, i, 8:16], tv[:, i, 8:16], tmp[:, i % 4, :]), t3[n])
                yield 3.0
                cm = work[:, 512 * g:512 * g + 512]
                cand = cm.rearrange("p (h i j) -> p h i j", h=2, i=16)
                cflat = cm.rearrange("p (h c) -> p h c", h=2)
                tvh = work[:, 4096 + 64 * g:4160 + 64 * g].rearrange("p (h t k) -> p h t k", h=2, t=2)
                tf = work[:, 4608 + 64 * g:4672 + 64 * g]
                tfh = tf.rearrange("p (h t k) -> p h t k", h=2, t=2)
                V(lambda e, tf=tf, g=g: e.tensor_copy(tf, work[:, 4352 + 64 * g:4416 + 64 * g].bitcast(U32)), t)
                t = V(lambda e, cand=cand, tvh=tvh: e.tensor_tensor(
                    cand, tvh[:, :, 0, :].unsqueeze(3).to_broadcast([128, 2, 16, 16]),
                    tvh[:, :, 1, :].unsqueeze(2).to_broadcast([128, 2, 16, 16]), ALU.add))
                top = work[:, 4864 + 32 * g:4896 + 32 * g].rearrange("p (h k) -> p h k", h=2)
                pos = work[:, 4992 + 32 * g:5024 + 32 * g].bitcast(U32)
                posh = pos.rearrange("p (h k) -> p h k", h=2)
                ctm = work[:, 5120:5632]
                ct = ctm.rearrange("p (h c) -> p h c", h=2)
                R = range(2)
                t1 = [V(lambda e, i=i, top=top, cflat=cflat: e.max(top[:, i, 0:8], cflat[:, i, :]), t) for i in R]
                for i in R:
                    V(lambda e, i=i, top=top, cflat=cflat, posh=posh: e.max_index(
                        posh[:, i, 0:8], top[:, i, 0:8], cflat[:, i, :]), t1[i])
                yield 2.5
                t2 = [V(lambda e, i=i, top=top, cflat=cflat, ct=ct: e.match_replace(
                    ct[:, i, :], top[:, i, 0:8], cflat[:, i, :], LOW)) for i in R]
                t3 = [V(lambda e, i=i, top=top, ct=ct: e.max(top[:, i, 8:16], ct[:, i, :]), t2[i]) for i in R]
                for i in R:
                    t = V(lambda e, i=i, top=top, ct=ct, posh=posh: e.max_index(
                        posh[:, i, 8:16], top[:, i, 8:16], ct[:, i, :]), t3[i])
                yield 2.5
                ga = sel_g[:, 128 * tile + 32 * g:128 * tile + 32 * g + 32].rearrange("p (h k) -> p h k", h=2)
                s8 = sm(4)
                tg = V(lambda e, ga=ga, top=top: e.tensor_tensor(ga, top, top[:, :, 0:1].to_broadcast([128, 2, 16]),
                                                                 ALU.subtract))
                tg = A(lambda e, ga=ga: e.activation(ga, ga, ACT.Exp), tg)
                pp, pf, ee, ef = (work[:, 2048 + 512 * g + 64 * q:2112 + 512 * g + 64 * q] for q in range(4))
                pp = pp.bitcast(U32)
                V(lambda e, pp=pp, pos=pos: e.tensor_scalar(pp[:, 0:32], pos, 4, None, ALU.logical_shift_right), t)
                t = V(lambda e, pp=pp, pos=pos: e.tensor_scalar(pp[:, 32:64], pos, 15, None, ALU.bitwise_and))
                t = V(lambda e, pp=pp, pf=pf: e.tensor_copy(pf, pp), t)
                eq = ctm.rearrange("p (n i) -> p n i", i=16)
                eqh = ctm.rearrange("p (h k i) -> p h k i", h=2, i=16)
                for s_ in range(2):
                    t = V(lambda e, s_=s_, eq=eq, pf=pf: e.tensor_tensor(
                        eq, pf[:, 32 * s_:32 * s_ + 32].unsqueeze(2).to_broadcast([128, 32, 16]),
                        iota.unsqueeze(1).to_broadcast([128, 32, 16]), ALU.is_equal), t)
                    t = V(lambda e, s_=s_, eqh=eqh, tfh=tfh: e.tensor_tensor(
                        eqh, eqh, tfh[:, :, s_, :].unsqueeze(2).to_broadcast([128, 2, 16, 16]), ALU.mult), t)
                    t = V(lambda e, s_=s_, eq=eq, ee=ee: e.tensor_reduce(ee[:, 32 * s_:32 * s_ + 32], eq, AX.X,
                                                                         ALU.add), t)
                    yield 2.5
                t = V(lambda e, ef=ef, ee=ee: e.scalar_tensor_tensor(ef[:, 0:32], ee[:, 0:32], 128.0, ee[:, 32:64],
                                                                     ALU.mult, ALU.add), t)
                if l:
                    t = V(lambda e, ef=ef: e.tensor_scalar(ef[:, 0:32], ef[:, 0:32], float(16384 * l), None,
                                                           ALU.add), t)
                ic = 128 * tile + 32 * g
                V(lambda e, ef=ef, ic=ic: e.tensor_copy(sel_idx[:, ic:ic + 32], ef[:, 0:32]), t)
                tg = V(lambda e, s8=s8, ga=ga: e.tensor_reduce(s8[:, 0:2], ga, AX.X, ALU.add), tg)
                tg = V(lambda e, s8=s8: e.reciprocal(s8[:, 2:4], s8[:, 0:2]), tg)
                tg = V(lambda e, s8=s8, ga=ga: e.tensor_tensor(ga, ga, s8[:, 2:4].unsqueeze(2).to_broadcast([128, 2, 16]),
                                                          ALU.mult), tg)
                chosen[(tile, l, g)] = tg
                yield 0.5

            picking = iter(())
            for g in range(4):
                for units in project([tile], lhsD, None, a["peer_w_q_2"][l], D, [(512 * g, 512)], ev):
                    yield units
                    for _, units in zip(range(4), picking):
                        yield units
                yield from picking
                b = banks.take()
                for j in range(4):
                    i = 4 * g + j
                    t = T(lambda e, b=b, i=i, j=j: e.matmul(b.ap[:, 128 * j:128 * j + 128], qT[:, i, :],
                          kyT[:, i, :], start=True, stop=True), b.free, turned[g], inc=(j == 3))
                picking = pick(g, b, t)
            yield from picking
            flip[1] = 4
            dense_bar()

        chosen = {}
        yfree = [None]

        def gather(table, idx, tok):
            s = gslots.take()
            t = G.dma(lambda e: e.indirect_dma_start(out=s.ap, out_offset=None, in_=table,
                      in_offset=bass.IndirectOffsetOnAxis(ap=idx, axis=0)), s, s.free, tok)
            return s, t

        def experts():
            rounds = [(l, tile, hd) for l in range(2) for tile in range(2) for hd in range(8)]
            tw = None
            for n_, (now, past) in enumerate(zip(rounds + [None], [None] + rounds)):
                for j in range(16):
                    if now:
                        l, tile, hd = now
                        c = 128 * tile + 16 * hd + j
                        s, t = gather(utab, sel_idx[:, c:c + 1], chosen[(tile, l, hd // 2)])
                        tu = V(lambda e, s=s, c=c, tile=tile: e.tensor_tensor_reduce(
                            s.ap, s.ap, h[tile], 1.0, 0.0, ALU.mult, ALU.add, acts[:, c:c + 1]), t, beside=True)
                        s.free = [tu]
                        yield
                    if past:
                        l, tile, hd = past
                        c = 128 * tile + 16 * hd + j
                        s, t = gather(vtab, sel_idx[:, c:c + 1], None)
                        d = dslots.take()
                        td = A(lambda e, d=d, c=c: e.activation(d.ap, ident, ACT.Copy, scale=acts[:, c:c + 1]),
                               tw, d.free, beside=True)
                        st, sp = (hd == 0 and j == 0), (hd == 7 and j == 15)
                        for n in range(2):
                            m = T(lambda e, d=d, s=s, n=n, st=st, sp=sp: e.matmul(ybank[n], d.ap,
                                  s.ap[:, 512 * n:512 * n + 512], start=st, stop=sp), td, t, yfree[0], inc=(n == 1),
                                  beside=True)
                        d.free = [m]
                        s.free = [m]
                        if sp:
                            for n in range(2):
                                xn = x[tile][:, 512 * n:512 * n + 512]
                                t = V(lambda e, n=n, xn=xn: e.tensor_tensor(xn, ybank[n], xn, ALU.add), m,
                                      beside=True)
                            yfree[0] = t
                            xtok[tile] = t
                        yield
                if now:
                    l, tile, hd = now
                    c0 = 128 * tile + 16 * hd
                    t = A(lambda e, c0=c0: e.activation(acts[:, c0:c0 + 16], acts[:, c0:c0 + 16], ACT.Gelu), tu,
                          beside=True)
                    tw = V(lambda e, c0=c0: e.tensor_tensor(acts[:, c0:c0 + 16], acts[:, c0:c0 + 16],
                           sel_g[:, c0:c0 + 16], ALU.mult), t, beside=True)

        def final(tile):
            t = norm(h[tile], x[tile], gain[4], D, h[tile], xtok[tile])
            S.dma(lambda e: e.dma_start(out[0, 128 * tile:128 * tile + 128, :], h[tile]), outs, t)

        def dense(*gens):
            for g in gens:
                yield from g

        fast = experts()
        steps = [0]

        def upto(n):
            while steps[0] < n:
                steps[0] += 1
                if next(fast, "end") == "end":
                    break

        def together(until, total, slow):
            first, spent = steps[0], 0.0
            for units in slow:
                spent += units or 1.0
                upto(min(until, first + int((until - first) * spent / total)))
            upto(until)

        def ends(r):
            return 16 + 32 * r

        hy = hybrid(0, tnorm)
        for _ in range(3):
            next(hy)
        xtok[1] = add_y(1, gt_f, *y_scale(1))
        run(hy)
        c00 = choose(0, 0)
        while (0, 0, 0) not in chosen:
            next(c00)
        together(ends(7) , W[0], dense(c00, hybrid(1), choose(1, 0)))
        upto(ends(8))
        together(ends(15), W[1], dense(mla(0), choose(0, 1)))
        upto(ends(16))
        together(ends(23), W[2], dense(mla(1), choose(1, 1)))
        upto(ends(24))
        final(0)
        upto(10 ** 6)
        final(1)
        S.wait((id(outs), outs.sem, outs.count))

        block = ctx.enter_context(nc.Block())

        @block.sync
        def _(eng):
            S.emit(eng)

        @block.vector
        def _(eng):
            V.emit(eng)

        @block.scalar
        def _(eng):
            A.emit(eng)

        @block.tensor
        def _(eng):
            T.emit(eng)

        @block.gpsimd
        def _(eng):
            G.emit(eng)


def shape_constants():
    c = np.zeros((128, C_END), np.float32)
    c[:, C_ID:C_ID + 128] = np.eye(128, dtype=np.float32)
    t = (128 * np.arange(2)[None, :, None] + np.arange(128)[:, None, None])
    s = np.arange(256)[None, None, :]
    d = t - s
    m = np.zeros((128, 4, 2, 256), np.float32)
    for g, ok in enumerate(((d >= 0) & (d <= 128), (d >= 0) & (d % 4 == 0), (d >= 0) & (d % 16 == 0), d >= 0)):
        m[:, g] = np.where(ok, 0.0, NEG)
    c[:, C_MASK:C_MASK + 2048] = m.reshape(128, 2048)
    f8 = np.float32(500000.0) ** (-np.arange(0, 16, 2, dtype=np.float32) / np.float32(16))
    f32_ = np.float32(1) / (np.float32(10000.0) ** (np.arange(0, 64, 2, dtype=np.float32) / np.float32(64)))
    f16 = np.float32(1) / (np.float32(10000.0) ** (np.arange(0, 32, 2, dtype=np.float32) / np.float32(32)))
    c[:, C_FREQ:C_FREQ + 112] = np.concatenate([f8, f8, f32_, f32_, f16, f16])
    c[:, C_SGN:C_SGN + 112] = np.concatenate([v * np.ones(n) for n in (8, 32, 16) for v in (-1, 1)])
    c[:, C_IOTA:C_IOTA + 16] = np.arange(16)
    tt, sx = np.arange(256)[None, :], np.arange(256)[:, None]
    band = np.zeros((256, 4, 256), np.float32)
    for g, w in enumerate((2, 4, 8, 16)):
        inside = (sx <= tt) & (sx > tt - w)
        band[:, g] = inside / np.minimum(tt + 1, w) - (sx == tt)
    band = band.reshape(2, 128, 4, 256).transpose(1, 0, 2, 3).reshape(128, 2048)
    return {"consts": c, "pool_band": np.ascontiguousarray(band)}


_INS = ["x", "c", "positions", "w_ada", "b_ada", "g_pre_mix", "g_post_mix", "g_pre_ffn", "g_post_ffn", "w_in",
        "w_pool", "b_pool", "pool_scale", "w_out", "w_up", "conv_w", "conv_b", "w_down", "positions_2",
        "attn_norm_2", "ffn_norm_2", "final_norm_2", "hyb_w_in_2", "hyb_w_out_2", "mla_w_in_2", "mla_q_norm_2",
        "mla_kv_norm_2", "mla_w_uq_2", "mla_w_ukv_2", "mla_w_out_2", "peer_w_q_2", "peer_sub_keys_2", "peer_u_2",
        "peer_v_2"]


def kernel(**inputs):
    import concourse.bacc as _bacc
    from concourse import mybir as _mybir
    from concourse.bass_utils import run_bass_kernel_spmd as _run

    nc = _bacc.Bacc("TRN2", target_bir_lowering=False, num_devices=1)
    arrays, args = {}, {}
    given = {n: inputs[n] for n in _INS if n[:9] != "positions"}
    given["pos"] = np.concatenate([np.asarray(inputs[n]).reshape(2, 128).T for n in ("positions", "positions_2")], 1)
    given.update(shape_constants())
    for name, value in given.items():
        v = np.ascontiguousarray(value)
        arrays[f"in_{name}_dram"] = v
        args[name] = nc.dram_tensor(f"in_{name}_dram", v.shape, _mybir.dt.from_np(v.dtype),
                                    kind="ExternalInput").ap()
    out = nc.dram_tensor("out_0_dram", (1, 256, 1024), _mybir.dt.float32, kind="ExternalOutput").ap()
    program(nc, args, out)
    r = _run(nc, [arrays], core_ids=[0])
    return r.results[0]["out_0_dram"]
```
